# Optimizing a Trainium2 kernel written in Bass

```python
import math
import jax, jax.numpy as jnp
from jax import lax
import numpy as np

D_MODEL = 1024
BATCH = 1
SEQ = 1024
DEPTH = 2

CHUNK = 64
N_META = 16
HEAD_DIM = 64
EPS = 1e-6
SB_HEADS = D_MODEL // 2 // HEAD_DIM
SB_WIDTH = SB_HEADS * HEAD_DIM
SB_BLOCK = 128
SSM_GROUP = 16
SSM_WIDTH = D_MODEL // 2
SSM_GROUPS = SSM_WIDTH // SSM_GROUP
SSM_STATE = 64
EVEN_IN = 4 * SB_WIDTH + 2 * SSM_WIDTH
EVEN_MIX = SB_WIDTH + SSM_WIDTH
SWA_HEADS = D_MODEL // HEAD_DIM
SWA_KV_HEADS = SWA_HEADS // 8
SWA_WIDTH = SWA_HEADS * HEAD_DIM
SWA_KV_WIDTH = SWA_KV_HEADS * HEAD_DIM
SWA_WINDOW = 128
WINDOW_CHUNKS = SWA_WINDOW // CHUNK
ODD_IN = 2 * SWA_WIDTH + 2 * SWA_KV_WIDTH
N_EVEN = (DEPTH + 1) // 2
N_ODD = DEPTH // 2

kernel_name = "chunk_causal_hybrid_sb_s5_swa"

def _rmsnorm(x, g):
    xf = x.astype(jnp.float32)
    r = lax.rsqrt(jnp.mean(xf * xf, axis=-1, keepdims=True) + EPS)
    return (xf * r).astype(x.dtype) * g

def _stick_breaking(q, k, v):
    L = q.shape[1]
    scale = HEAD_DIM ** -0.5
    starts = [0] + list(range(N_META, L, SB_BLOCK))
    ends = starts[1:] + [L]
    outs = []
    for s0, s1 in zip(starts, ends):
        qb = q[:, s0:s1]
        kp, vp = k[:, :s1], v[:, :s1]
        z = jnp.einsum('bqhd,bkhd->bhqk', qb, kp).astype(jnp.float32) * scale
        mask = jnp.arange(s1)[None, :] < jnp.arange(s0, s1)[:, None]
        log_beta = jax.nn.log_sigmoid(z)
        log_1m = jnp.where(mask, jax.nn.log_sigmoid(-z), 0.0)
        tail = lax.cumsum(log_1m, axis=3, reverse=True) - log_1m
        w = jnp.where(mask, jnp.exp(log_beta + tail), 0.0)
        outs.append(jnp.einsum('bhqk,bkhd->bqhd', w.astype(v.dtype), vp))
    return jnp.concatenate(outs, axis=1)

def _s5_scan(u, log_dt, a_re, a_im, b_re, b_im, c_re, c_im, d_skip):
    bsz, L, _ = u.shape
    f32 = jnp.float32
    uf = u.astype(f32).reshape(bsz, L, SSM_GROUPS, SSM_GROUP)
    dt = jnp.exp(log_dt.astype(f32))[:, None]
    ar = jnp.minimum(a_re.astype(f32), -1e-4)
    ai = a_im.astype(f32)
    mag = jnp.exp(dt * ar)
    abar_re = mag * jnp.cos(dt * ai)
    abar_im = mag * jnp.sin(dt * ai)
    den = ar * ar + ai * ai
    xr = abar_re - 1.0
    f_re = ((xr * ar + abar_im * ai) / den)[..., None]
    f_im = ((abar_im * ar - xr * ai) / den)[..., None]
    br, bi = b_re.astype(f32), b_im.astype(f32)
    bb_re = f_re * br - f_im * bi
    bb_im = f_re * bi + f_im * br
    h_re = jnp.einsum('blgc,gnc->blgn', uf, bb_re)
    h_im = jnp.einsum('blgc,gnc->blgn', uf, bb_im)
    at_re = jnp.broadcast_to(abar_re, h_re.shape)
    at_im = jnp.broadcast_to(abar_im, h_im.shape)

    def combine(e1, e2):
        a1r, a1i, b1r, b1i = e1
        a2r, a2i, b2r, b2i = e2
        return (a2r * a1r - a2i * a1i, a2r * a1i + a2i * a1r,
                a2r * b1r - a2i * b1i + b2r, a2r * b1i + a2i * b1r + b2i)

    _, _, s_re, s_im = lax.associative_scan(combine, (at_re, at_im, h_re, h_im), axis=1)
    y = (jnp.einsum('blgn,gcn->blgc', s_re, c_re.astype(f32))
         - jnp.einsum('blgn,gcn->blgc', s_im, c_im.astype(f32))
         + d_skip.astype(f32) * uf)
    return y.reshape(bsz, L, SSM_WIDTH).astype(u.dtype)

def _alibi_slopes(n_heads):
    return jnp.exp2(-8.0 * jnp.arange(1, n_heads + 1, dtype=jnp.float32) / n_heads)

def _softmax_with_sink(s, sink):
    m = jnp.maximum(jnp.max(s, axis=-1, keepdims=True), sink)
    p = jnp.exp(s - m)
    return p / (jnp.sum(p, axis=-1, keepdims=True) + jnp.exp(sink - m))

def _band(xc):
    n_chunks = xc.shape[1]
    parts = []
    for j in range(WINDOW_CHUNKS - 1, -1, -1):
        pad = [(0, 0)] * xc.ndim
        pad[1] = (j, 0)
        parts.append(jnp.pad(xc, pad)[:, :n_chunks])
    return jnp.concatenate(parts, axis=2)

def _swa_with_sinks(q, k, v, sinks):
    bsz, L = q.shape[0], q.shape[1]
    f32 = jnp.float32
    n_chunks = (L - N_META) // CHUNK
    grp = SWA_HEADS // SWA_KV_HEADS
    scale = HEAD_DIM ** -0.5
    band = WINDOW_CHUNKS * CHUNK
    slopes = _alibi_slopes(SWA_HEADS).reshape(SWA_KV_HEADS, grp)
    sink = sinks.astype(f32).reshape(SWA_KV_HEADS, grp)
    km, vm = k[:, :N_META], v[:, :N_META]
    qm = q[:, :N_META].reshape(bsz, N_META, SWA_KV_HEADS, grp, HEAD_DIM)
    s_mm = jnp.einsum('bqhgd,bkhd->bhgqk', qm, km).astype(f32) * scale
    p_mm = _softmax_with_sink(s_mm, sink[None, :, :, None, None])
    o_meta = jnp.einsum('bhgqk,bkhd->bqhgd', p_mm.astype(v.dtype), vm)
    qc = q[:, N_META:].reshape(bsz, n_chunks, CHUNK, SWA_KV_HEADS, grp, HEAD_DIM)
    kb = _band(k[:, N_META:].reshape(bsz, n_chunks, CHUNK, SWA_KV_HEADS, HEAD_DIM))
    vb = _band(v[:, N_META:].reshape(bsz, n_chunks, CHUNK, SWA_KV_HEADS, HEAD_DIM))
    qi = jnp.arange(CHUNK, dtype=f32)[:, None]
    ki = jnp.arange(band, dtype=f32)[None, :]
    dist = jnp.abs(qi - ki + float(band - CHUNK))
    key_frame = (jnp.arange(n_chunks)[:, None] - (WINDOW_CHUNKS - 1)) * CHUNK + jnp.arange(band)[None, :]
    valid = key_frame >= 0
    s_band = (jnp.einsum('bcqhgd,bckhd->bchgqk', qc, kb).astype(f32) * scale
              - slopes[:, :, None, None] * dist)
    s_band = jnp.where(valid[None, :, None, None, None, :], s_band, -jnp.inf)
    s_meta = jnp.einsum('bcqhgd,bkhd->bchgqk', qc, km).astype(f32) * scale
    p = _softmax_with_sink(jnp.concatenate([s_meta, s_band], axis=-1),
                           sink[None, None, :, :, None, None]).astype(v.dtype)
    o_frames = (jnp.einsum('bchgqk,bkhd->bcqhgd', p[..., :N_META], vm)
                + jnp.einsum('bchgqk,bckhd->bcqhgd', p[..., N_META:], vb))
    return jnp.concatenate([o_meta.reshape(bsz, N_META, SWA_WIDTH),
                            o_frames.reshape(bsz, n_chunks * CHUNK, SWA_WIDTH)], axis=1)

def _even_layer(h, norm_g, w_in, q_g, k_g, log_dt, a_re, a_im, b_re, b_im,
                c_re, c_im, d_skip, w_glu, b_glu, w_out):
    bsz, L, _ = h.shape
    z = _rmsnorm(h, norm_g) @ w_in
    q, k, v, g_sb, u, g_ssm = jnp.split(
        z, [SB_WIDTH, 2 * SB_WIDTH, 3 * SB_WIDTH, 4 * SB_WIDTH, 4 * SB_WIDTH + SSM_WIDTH], axis=-1)
    q = _rmsnorm(q.reshape(bsz, L, SB_HEADS, HEAD_DIM), q_g)
    k = _rmsnorm(k.reshape(bsz, L, SB_HEADS, HEAD_DIM), k_g)
    v = v.reshape(bsz, L, SB_HEADS, HEAD_DIM)
    y_sb = _stick_breaking(q, k, v).reshape(bsz, L, SB_WIDTH) * jax.nn.silu(g_sb)
    y = jax.nn.gelu(_s5_scan(u, log_dt, a_re, a_im, b_re, b_im, c_re, c_im, d_skip))
    y = y * jax.nn.sigmoid(y @ w_glu + b_glu)
    y_ssm = y * jax.nn.silu(g_ssm)
    return jnp.concatenate([y_sb, y_ssm], axis=-1) @ w_out

def _odd_layer(h, norm_g, w_in, q_g, k_g, sinks, w_out):
    bsz, L, _ = h.shape
    z = _rmsnorm(h, norm_g) @ w_in
    q, k, v, gate = jnp.split(z, [SWA_WIDTH, SWA_WIDTH + SWA_KV_WIDTH, SWA_WIDTH + 2 * SWA_KV_WIDTH], axis=-1)
    q = _rmsnorm(q.reshape(bsz, L, SWA_HEADS, HEAD_DIM), q_g)
    k = _rmsnorm(k.reshape(bsz, L, SWA_KV_HEADS, HEAD_DIM), k_g)
    v = v.reshape(bsz, L, SWA_KV_HEADS, HEAD_DIM)
    o = _swa_with_sinks(q, k, v, sinks)
    return (o * jax.nn.silu(gate)) @ w_out

def setup_inputs(seed: int = 0) -> dict:
    key = jax.random.key(seed)
    ks = jax.random.split(key, 24)
    nrm = jax.random.normal
    f32 = jnp.float32
    n_idx = jnp.arange(SSM_STATE, dtype=f32)
    return {
        "x": nrm(ks[0], (BATCH, SEQ, D_MODEL), f32),
        "meta_tokens": nrm(ks[1], (N_META, D_MODEL), f32),
        "ev_norm": 1.0 + 0.01 * nrm(ks[2], (N_EVEN, D_MODEL), f32),
        "ev_w_in": nrm(ks[3], (N_EVEN, D_MODEL, EVEN_IN), f32) * D_MODEL ** -0.5,
        "ev_q_norm": 1.0 + 0.01 * nrm(ks[4], (N_EVEN, HEAD_DIM), f32),
        "ev_k_norm": 1.0 + 0.01 * nrm(ks[5], (N_EVEN, HEAD_DIM), f32),
        "ev_log_dt": jax.random.uniform(ks[6], (N_EVEN, SSM_GROUPS), f32, math.log(0.001), math.log(0.1)),
        "ev_a_re": -0.5 + 0.01 * nrm(ks[7], (N_EVEN, SSM_GROUPS, SSM_STATE), f32),
        "ev_a_im": math.pi * n_idx + 0.01 * nrm(ks[8], (N_EVEN, SSM_GROUPS, SSM_STATE), f32),
        "ev_b_re": nrm(ks[9], (N_EVEN, SSM_GROUPS, SSM_STATE, SSM_GROUP), f32) * (2 * SSM_GROUP) ** -0.5,
        "ev_b_im": nrm(ks[10], (N_EVEN, SSM_GROUPS, SSM_STATE, SSM_GROUP), f32) * (2 * SSM_GROUP) ** -0.5,
        "ev_c_re": nrm(ks[11], (N_EVEN, SSM_GROUPS, SSM_GROUP, SSM_STATE), f32) * SSM_STATE ** -0.5,
        "ev_c_im": nrm(ks[12], (N_EVEN, SSM_GROUPS, SSM_GROUP, SSM_STATE), f32) * SSM_STATE ** -0.5,
        "ev_d": nrm(ks[13], (N_EVEN, SSM_GROUPS, SSM_GROUP), f32),
        "ev_w_glu": nrm(ks[14], (N_EVEN, SSM_WIDTH, SSM_WIDTH), f32) * SSM_WIDTH ** -0.5,
        "ev_b_glu": 0.01 * nrm(ks[15], (N_EVEN, SSM_WIDTH), f32),
        "ev_w_out": nrm(ks[16], (N_EVEN, EVEN_MIX, D_MODEL), f32) * EVEN_MIX ** -0.5,
        "od_norm": 1.0 + 0.01 * nrm(ks[17], (N_ODD, D_MODEL), f32),
        "od_w_in": nrm(ks[18], (N_ODD, D_MODEL, ODD_IN), f32) * D_MODEL ** -0.5,
        "od_q_norm": 1.0 + 0.01 * nrm(ks[19], (N_ODD, HEAD_DIM), f32),
        "od_k_norm": 1.0 + 0.01 * nrm(ks[20], (N_ODD, HEAD_DIM), f32),
        "od_sinks": 0.5 * nrm(ks[21], (N_ODD, SWA_HEADS), f32),
        "od_w_out": nrm(ks[22], (N_ODD, SWA_WIDTH, D_MODEL), f32) * SWA_WIDTH ** -0.5,
    }

def reference(x, meta_tokens, ev_norm, ev_w_in, ev_q_norm, ev_k_norm, ev_log_dt,
              ev_a_re, ev_a_im, ev_b_re, ev_b_im, ev_c_re, ev_c_im, ev_d,
              ev_w_glu, ev_b_glu, ev_w_out, od_norm, od_w_in, od_q_norm,
              od_k_norm, od_sinks, od_w_out):
    bsz = x.shape[0]
    meta = jnp.broadcast_to(meta_tokens[None].astype(x.dtype), (bsz, N_META, D_MODEL))
    h = jnp.concatenate([meta, x], axis=1)
    for layer in range(DEPTH):
        i = layer // 2
        if layer % 2 == 0:
            h = h + _even_layer(h, ev_norm[i], ev_w_in[i], ev_q_norm[i], ev_k_norm[i],
                                ev_log_dt[i], ev_a_re[i], ev_a_im[i], ev_b_re[i], ev_b_im[i],
                                ev_c_re[i], ev_c_im[i], ev_d[i], ev_w_glu[i], ev_b_glu[i],
                                ev_w_out[i])
        else:
            h = h + _odd_layer(h, od_norm[i], od_w_in[i], od_q_norm[i], od_k_norm[i],
                               od_sinks[i], od_w_out[i])
    return h[:, N_META:]


_drawn_inputs = setup_inputs


def setup_inputs(seed=0):
    import zlib

    import numpy as np

    out = dict(_drawn_inputs(seed))
    spreads = {}
    factors = {'ev_norm': 8.0,
     'ev_q_norm': 8.0,
     'ev_k_norm': 8.0,
     'ev_log_dt': 4.444,
     'ev_a_re': 64.0,
     'ev_a_im': 4.345,
     'ev_b_re': 17.919,
     'ev_b_im': 17.812,
     'ev_c_re': 19.407,
     'ev_c_im': 20.974,
     'ev_b_glu': 8.0,
     'od_norm': 8.0,
     'od_q_norm': 8.0,
     'od_k_norm': 8.0,
     'od_sinks': 8.0}
    for name, (base, spread) in spreads.items():
        noise = np.random.default_rng([zlib.crc32(name.encode()), seed]).standard_normal(out[name].shape)
        drawn = base * np.exp(spread * noise) if base else spread * noise
        out[name] = __import__('jax').numpy.asarray(drawn.astype(out[name].dtype))
    for name, factor in factors.items():
        out[name] = (out[name] * factor).astype(out[name].dtype)
    return out
```

```python
from contextlib import ExitStack

import concourse.bass as bass
from concourse import mybir

ALU = mybir.AluOpType
ACT = mybir.ActivationFunctionType
F32 = mybir.dt.float32
F32R = mybir.dt.float32r
BF16 = mybir.dt.bfloat16
I32 = mybir.dt.int32
AX_X = mybir.AxisListType.X

P = 128
D = 1024
KD = D // P
META = 16
SEQ = 1024
L = META + SEQ
NT = 1 + SEQ // P
HD = 64
EPS = 1e-6
BANK = 512

NPAIR = 4
G, GC, NST = 32, 16, 64
G2 = G // 2
TC = 8
NCH = L // TC
MCH = META // TC
LOG_SCALE = 10
TAYLOR = 7

CHUNKS = [(0, 400), (400, 784), (784, 1040)]
SEC = 256
BIG = 1e30


def tile_cols(t):
    return (0, META) if t == 0 else (META + P * (t - 1), P)


def bc(ap, axis, n):
    v = ap.unsqueeze(axis)
    shape = list(v.shape)
    shape[axis] = n
    return v.broadcast_to(tuple(shape))


class Ring:

    def __init__(self, sems, banks, emptied_by):
        self.filled, self.emptied = sems["filled"], sems
        self.banks, self.by = banks, emptied_by

    def bank(self, n):
        return self.banks[n % len(self.banks)]

    def wait_free(self, pe, n):
        m = n - len(self.banks)
        if m >= 0:
            e = self.by[m]
            pe.wait_ge(self.emptied[e], self.by[:m + 1].count(e))

    def wait_filled(self, eng, n):
        eng.wait_ge(self.filled, n + 1)


class Chain:

    def __init__(self, eng, sem):
        self.eng, self.sem, self.n = eng, sem, 0

    def link(self, ins):
        self.n += 1
        ins.then_inc(self.sem, 1)
        self.eng.wait_ge(self.sem, self.n)


class K:
    pass


def plan_memory(nc, ctx):
    m = K()

    def sb(name, cols, dt=F32, parts=P):
        return ctx.enter_context(nc.sbuf_tensor(name, [parts, cols], dt))

    m.ident = sb("ident", P)
    m.tri = sb("tri", P)
    m.ones = sb("ones", P)
    m.headmean = sb("headmean", P)
    m.kvcopy = sb("kvcopy", 2 * P)
    m.identb = sb("identb", P, BF16)
    m.negmask = sb("negmask", P, BF16)
    m.sm = sb("sm", 960)
    m.wst = sb("wst", 2 * KD * SEC)
    m.bank = [ctx.enter_context(nc.psum_tensor(f"bank{i}", [P, BANK], F32)) for i in range(2)]
    m.wide = [ctx.enter_context(nc.psum_tensor(f"wide{i}", [P, 2 * BANK], F32)) for i in range(3)]
    m.banks = [m.wide[i][:, h * BANK:(h + 1) * BANK] for i in range(3) for h in range(2)] + \
              [b[:, :] for b in m.bank]
    m.small_at = 0

    def small(n):
        m.small_at += n
        assert m.small_at <= 960
        return m.sm[:, m.small_at - n:m.small_at]

    m.gain = {n: small(KD) for n in ("ev", "od")}
    m.head_gain = {n: small(1) for n in ("evq", "evk", "odq", "odk")}
    m.eps = small(1)
    m.bglu = small(4)
    m.sinks, m.nsinks, m.sinks_in = small(16), small(16), small(16)
    m.ss = small(16)
    m.rstd = small(16)
    m.msq = small(16)
    m.small = small
    return m


class Area:

    def __init__(self, nc):
        self.nc, self.ctx = nc, ExitStack()

    def take(self, name, cols, dt=F32):
        return self.ctx.enter_context(self.nc.sbuf_tensor(name, [P, cols], dt))[:, :]

    def close(self):
        self.ctx.close()


HEAD = 8 * L + NT * 512


def split_tiles(act, dve, pool, src, hi, lo, on_act, sems):
    hi_act, hi_dve, lo_pool, lo_dve = sems
    n = 0
    for k in range(KD):
        if k in on_act:
            n += 1
            if act:
                act.activation(hi[:, k], src[:, k], ACT.Copy).then_inc(hi_act, 1)
            if pool:
                pool.wait_ge(hi_act, n)
                pool.tensor_tensor(lo[:, k], src[:, k], hi[:, k].bitcast(F32), ALU.subtract).then_inc(lo_pool, 1)
        elif dve:
            dve.tensor_copy(hi[:, k], src[:, k]).then_inc(hi_dve, 1)
            dve.wait_ge(hi_dve, k + 1 - n)
            dve.tensor_tensor(lo[:, k], src[:, k], hi[:, k].bitcast(F32), ALU.subtract).then_inc(lo_dve, 1)


ON_ACT = (0, 2, 4)


def wait_split(pe, k, sems):
    n = sum(1 for j in ON_ACT if j <= k)
    pe.wait_ge(sems[2], n)
    if k + 1 - n:
        pe.wait_ge(sems[3], k + 1 - n)


def split_product(nc, out, lhs, rhs, nk=KD, before=None):
    for k in range(nk):
        if before:
            before(k)
        for n, (i, j) in enumerate(((0, 0), (0, 1), (1, 0))):
            ins = nc.tensor.matmul(out, lhs(k)[i], rhs(k)[j], start=(k == 0 and n == 0), stop=(k == nk - 1 and n == 2))
    return ins


def kernel_program(nc, a, out):
    ctx = ExitStack()
    with ctx:
        m = plan_memory(nc, ctx)
        made = [0]

        def sem(name):
            made[0] += 1
            return ctx.enter_context(nc.semaphore(f"{name}_{made[0]}"))

        def ring(banks, by):
            return Ring({k: sem(k) for k in ["filled"] + sorted(set(by))}, banks, by)

        m.sem, m.ring = sem, ring
        ctx.enter_context(nc.allow_non_contiguous_dma(reason="small per-feature parameters"))
        views(m, a)
        mixes = Area(nc)
        m.mix = mixes.take("mix", 8 * L)
        area = Area(nc)
        m.f1, m.xn, m.f2 = area.take("s5_a", HEAD), area.take("xn", KD * L), area.take("s5_b", 17056)
        m.xnT = m.xn.rearrange("p (k l) -> p k l", k=KD)
        m.mixT = m.mix.rearrange("p (k l) -> p k l", k=8)
        norm_stage(nc, m, a)
        s5_input_stage(nc, m, a)
        s5_stage(nc, m, a)
        area.close()
        qkv_area = Area(nc)
        m.qk, m.vrows = qkv_area.take("qk", 8 * L), qkv_area.take("vrows", NT * 512)
        area = Area(nc)
        split_area(m, area, 0)
        qkv_stage(nc, m, a, area)
        area.close()
        area = Area(nc)
        stick_breaking_stage(nc, m, a, area)
        area.close()
        qkv_area.close()
        mixes.close()

        mixes = Area(nc)
        m.mixlo = mixes.take("mix_lo0", 8 * L, F32R)
        area = Area(nc)
        even_out_stage(nc, m, a, area)
        area.close()
        mixes.close()
        mixes = Area(nc)
        m.mix = mixes.take("mix1", 8 * L)
        m.mixT = m.mix.rearrange("p (k l) -> p k l", k=8)
        head = Area(nc)
        m.qkv1 = head.take("qkv1", HEAD)
        area = Area(nc)
        split_area(m, area, 1)
        odd_in_stage(nc, m, a, area)
        area.close()
        area = Area(nc)
        window_stage(nc, m, a, area)
        area.close()
        head.close()
        mixes.close()
        mixes = Area(nc)
        m.mixlo = mixes.take("mix_lo1", 8 * L, F32R)
        area = Area(nc)
        odd_out_stage(nc, m, a, out, area)
        area.close()
        mixes.close()


def split_area(m, area, layer):
    m.xlo = area.take(f"xn_lo{layer}", KD * L, F32R).rearrange("p (k l) -> p k l", k=KD)
    m.xhi = area.take(f"xn_hi{layer}", KD * L, F32R).rearrange("p (k l) -> p k l", k=KD)
    m.whi = [area.take(f"w_hi{layer}{i}", KD * P, F32R).rearrange("p (k n) -> p k n", k=KD) for i in range(2)]
    m.wlo = [area.take(f"w_lo{layer}{i}", KD * P, F32R).rearrange("p (k n) -> p k n", k=KD) for i in range(2)]


def views(m, a):
    w0 = a["ev_w_in"][0].rearrange("(k p) n -> p k n", p=P)
    w1 = a["od_w_in"][0].rearrange("(k p) n -> p k n", p=P)
    sections = []

    def add(name, w, c0):
        sections.append((name, w[:, :, c0:c0 + SEC]))

    add("u0", w0, 2048), add("u1", w0, 2304)
    for s in range(2):
        add(f"gs{s}", w0, 2560 + SEC * s)
    for s in range(2):
        add(f"gb{s}", w0, 1536 + SEC * s)
    sections.append(("glu", a["ev_w_glu"][0].rearrange("(k p) n -> p k n", p=P)))
    for i, name in enumerate(("q0", "q1", "k0", "k1", "v0", "v1")):
        add(name, w0, SEC * i)
    wo = [a[n][0].rearrange("(k p) n -> p k n", p=P) for n in ("ev_w_out", "od_w_out")]
    for s in range(4):
        add(f"eo{s}", wo[0], SEC * s)
    add("okv", w1, 1024)
    for s in range(4):
        add(f"oq{s}", w1, SEC * s)
    for s in range(4):
        add(f"og{s}", w1, 1280 + SEC * s)
    for s in range(4):
        add(f"oo{s}", wo[1], SEC * s)
    m.sections = sections
    m.section_at = {n: i for i, (n, _) in enumerate(sections)}
    m.section_loaded = [m.sem("section_loaded") for _ in range(2)]
    m.section_end = {}
    m.sections_sent = 0


def section(m, name):
    i = m.section_at[name]
    k, n = m.sections[i][1].shape[1:]
    return m.wst[:, (i % 2) * KD * SEC:(i % 2 + 1) * KD * SEC].rearrange("p (k n) -> p k n", k=k)


def send_sections(m, sp, upto):
    while m.sections_sent <= min(upto, len(m.sections) - 1):
        i = m.sections_sent
        name, src = m.sections[i]
        if i >= 2:
            sp.wait_ge(*m.section_end[m.sections[i - 2][0]])
        sp.dma_start(section(m, name), src).then_inc(m.section_loaded[i % 2], 16)
        m.sections_sent += 1


def wait_section(m, pe, name):
    i = m.section_at[name]
    pe.wait_ge(m.section_loaded[i % 2], 16 * (i // 2 + 1))


def norm_stage(nc, m, a):
    f = m.f1
    rows = [f[:, 0:D]] + [m.mix[:, D * (t - 1):D * t] for t in range(1, NT)]
    row_loaded = [m.sem("row_loaded") for _ in range(NT)]
    consts, params = m.sem("consts"), m.sem("params")
    par = m.sem("par")
    junk = f[:, 2048:2048 + D]
    nfill = 2 * NT
    ring = m.ring(m.banks, ["dve"] * nfill)
    sq_done, ms_done, rt_done, rs_done, scaled = (m.sem(x) for x in ("sq_done", "ms_done", "rt_done", "rs_done", "scaled"))
    zi, chain = m.sem("zi"), m.sem("chain")

    with nc.Block() as block:
        @block.sync
        def _(sp):
            sp.dma_start(rows[0][0:META, :], a["meta_tokens"]).then_inc(row_loaded[0], 16)
            for t in range(1, NT):
                sp.dma_start(rows[t], a["x"][0, P * (t - 1):P * t, :]).then_inc(row_loaded[t], 16)
            send_sections(m, sp, 1)

        @block.gpsimd
        def _(pool):
            pool.memset(m.ident[:, :], 0.0).then_inc(zi, 1)
            pool.memset(m.identb[:, :], 0.0).then_inc(zi, 1)
            pool.memset(m.tri[:, :], -1.0).then_inc(zi, 1)
            pool.memset(m.negmask[:, :], -BIG).then_inc(zi, 1)
            pool.memset(m.ones[:, :], -1.0).then_inc(consts, 1)
            pool.wait_ge(zi, 4)
            for t in (m.ident, m.identb):
                pool.affine_select(out=t[:, :], in_=t[:, :], compare_op=ALU.not_equal, fill=1.0,
                                   base=0, pattern=[[-1, P]], channel_multiplier=1).then_inc(consts, 1)
            for t in (m.tri, m.negmask):
                pool.affine_select(out=t[:, :], in_=t[:, :], compare_op=ALU.is_ge, fill=0.0,
                                   base=0, pattern=[[-1, P]], channel_multiplier=1).then_inc(consts, 1)
            pool.wait_ge(consts, 5)

        @block.scalar
        def _(act):
            for n, src in (("ev", "ev_norm"), ("od", "od_norm")):
                act.dma_start(m.gain[n], a[src][0].rearrange("(k p) -> p k", p=P)).then_inc(params, 16)
            for n, src in (("evq", "ev_q_norm"), ("evk", "ev_k_norm"), ("odq", "od_q_norm"), ("odk", "od_k_norm")):
                for h in range(2):
                    act.dma_start(m.head_gain[n][HD * h:HD * h + HD, :],
                                  a[src][0].rearrange("(p o) -> p o", o=1)).then_inc(params, 16)
            act.dma_start(m.bglu, a["ev_b_glu"][0].rearrange("(k p) -> p k", p=P)).then_inc(params, 16)
            act.dma_start(m.sinks_in, a["od_sinks"][0:1, :].broadcast_to((P, 16))).then_inc(params, 16)
            act.wait_ge(chain, 1)
            for t in range(NT):
                n = tile_cols(t)[1]
                act.wait_ge(row_loaded[t], 16)
                act.activation(junk[0:n, :], rows[t][0:n, :], ACT.Square,
                               accum_out=m.ss[0:n, t:t + 1]).then_inc(sq_done, 1)
                act.wait_ge(ms_done, t + 1)
                act.activation(m.rstd[0:n, t:t + 1], m.msq[0:n, t:t + 1], ACT.Sqrt).then_inc(rt_done, 1)
                act.wait_ge(rs_done, t + 1)
                act.activation(rows[t][0:n, :], rows[t][0:n, :], ACT.Copy,
                               scale=m.rstd[0:n, t:t + 1]).then_inc(scaled, 1)

        @block.tensor
        def _(pe):
            pe.wait_ge(consts, 5)
            for t in range(NT):
                n = tile_cols(t)[1]
                pe.wait_ge(scaled, t + 1)
                for half in range(2):
                    transpose_half(nc, m, pe, ring, 2 * t + half, rows[t], n, half)

        @block.vector
        def _(dve):
            c = Chain(dve, chain)
            c.link(dve.memset(m.ss, 1.0))
            dve.memset(m.eps, EPS)
            dve.memset(m.headmean[:, :], 0.0)
            c.link(dve.memset(m.kvcopy[:, :], 0.0))
            for h in range(2):
                dve.memset(m.headmean[HD * h:HD * h + HD, HD * h:HD * h + HD], 1.0 / HD)
            dve.wait_ge(consts, 5)
            for v in range(2):
                for h in range(2):
                    dve.tensor_copy(m.kvcopy[:, P * v + HD * h:P * v + HD * h + HD], m.ident[:, HD * v:HD * v + HD])
            dve.wait_ge(params, 16 * 12)
            for n in ("evq", "odq"):
                c.link(dve.tensor_scalar(m.head_gain[n], m.head_gain[n], HD ** -0.5, None, ALU.mult))
            perm = m.sinks_in.rearrange("p (g h b) -> p g b h", g=4, b=2)
            dve.tensor_copy(m.sinks.rearrange("p (g b h) -> p g b h", g=4, b=2), perm)
            c.link(dve.tensor_scalar(m.nsinks.rearrange("p (g b h) -> p g b h", g=4, b=2), perm, -1.0, None, ALU.mult))
            for t in range(NT + 1):
                if t < NT:
                    n = tile_cols(t)[1]
                    rstd_steps(dve, m, t, n, sq_done, ms_done, rt_done, rs_done)
                if t >= 1:
                    empty_transposes(dve, m, ring, 2 * (t - 1), t - 1, "ev")


def rstd_steps(dve, m, t, n, sq_done, ms_done, rt_done, rs_done):
    dve.wait_ge(sq_done, t + 1)
    dve.tensor_scalar(m.msq[0:n, t:t + 1], m.ss[0:n, t:t + 1], 1.0 / D, EPS, ALU.mult, ALU.add).then_inc(ms_done, 1)
    dve.wait_ge(rt_done, t + 1)
    dve.reciprocal(m.rstd[0:n, t:t + 1], m.rstd[0:n, t:t + 1]).then_inc(rs_done, 1)


def transpose_half(nc, m, pe, ring, fill, row, n, half):
    ring.wait_free(pe, fill)
    for j in range(4):
        k = 4 * half + j
        last = nc.tensor.transpose(ring.bank(fill)[:, j * n:(j + 1) * n], row[0:n, P * k:P * k + P], m.ident[0:n, 0:n])
    last.then_inc(ring.filled, 1)


def empty_transposes(dve, m, ring, fill, t, gain):
    c0, n = tile_cols(t)
    for half in range(2):
        ring.wait_filled(dve, fill + half)
        dve.tensor_tensor(m.xnT[:, 4 * half:4 * half + 4, c0:c0 + n],
                          ring.bank(fill + half)[:, 0:4 * n].rearrange("p (k n) -> p k n", k=4),
                          bc(m.gain[gain][:, 4 * half:4 * half + 4], 2, n), ALU.mult).then_inc(ring.emptied["dve"], 1)


def row_product(nc, m, pe, out, cols, w, c0, c1, last_sem=None):
    for k in range(KD):
        ins = nc.tensor.matmul(out, m.xnT[:, k, cols], w[:, k, c0:c1], start=(k == 0), stop=(k == KD - 1))
    return ins


def col_product(nc, m, pe, out, lhs, rhs, nk=KD):
    for k in range(nk):
        ins = nc.tensor.matmul(out, lhs(k), rhs(k), start=(k == 0), stop=(k == nk - 1))
    return ins


def s5_views(m):
    at = [0, 0]

    def take(n, where=1):
        at[where] += n
        return (m.f1, m.f2)[where][:, at[where] - n:at[where]]

    m.urow = take(TC * SEC, 0).rearrange("p (g j c) -> p g j c", g=G2, j=TC)
    m.uj = take(G * NCH, 0).rearrange("p (g c) -> p g c", g=G)
    m.w1 = take(G2 * 2 * P, 0).rearrange("p (g r s) -> p g r s", g=G2, r=2)
    m.ca = take(2 * G2 * 9 * GC).rearrange("p (r g k c) -> p r g k c", r=2, g=G2, k=9)
    m.w3 = take(G * P).rearrange("p (g n) -> p g n", g=G)
    v = take(2 * G2 * (NCH + 1))
    m.v = v.rearrange("p (r g c) -> p r g c", r=2, g=G2)
    m.ba = v[:, 0:2 * G2 * TC * GC].rearrange("p (r g j c) -> p r g j c", r=2, g=G2, j=TC)
    ptab = take(2 * G2 * NCH)
    m.turn = ptab.rearrange("p (r g c) -> p r g c", r=2, g=G2)
    m.yT = ptab.rearrange("p (k l) -> p k l", k=4)
    m.tmp = take(2016, 0)
    m.radius = m.small(G2)


def s5_input_stage(nc, m, a):
    s5_views(m)
    mx = m.mix
    t4 = [mx[:, 1024 * i:1024 * i + 1024] for i in range(4)]
    zt = mx[0:GC, 0:4096].rearrange("p (g n) -> p g n", g=G)
    pt = [mx[:, 4096 + 576 * i:4096 + 576 * (i + 1)] for i in range(4)]
    braw = mx[:, 6400:6912].rearrange("p (r g c) -> p r g c", r=2, g=G2)
    craw = mx[:, 6912:7424].rearrange("p (r t s) -> p r t s", r=2, t=2)
    arow = mx[0:G2, 7424:7424 + 384].rearrange("p (i s) -> p i s", i=3)
    ldt = mx[0:G2, 7808:7810]
    um16 = mx[0:META, 7810:7810 + SEC]
    um2 = m.w3.rearrange("p g n -> p (g n)")[0:MCH, 0:TC * SEC].rearrange("p (g j c) -> p g j c", g=G2, j=TC)
    dcol = mx[0:GC, 8066:8066 + G]
    sm = mx[:, 8100:8320]

    small = [m.small(G2) for _ in range(12)]
    ar, ai, dt, zr, zi, er, ei, s1, s2, s3, s4, s5 = small
    pw = m.small(9 * 2 * G2).rearrange("p (k r g) -> p k r g", k=9, r=2)

    param_loaded, c_loaded, b_loaded, d_loaded = (m.sem(x) for x in ("param_loaded", "c_loaded", "b_loaded", "d_loaded"))
    um_evac, um_moved = m.sem("um_evac"), m.sem("um_moved")
    arow_ready, dt_ready, steps = m.sem("arow_ready"), m.sem("dt_ready"), m.sem("steps")
    power_ready, ba_ready, ca_ready, z_ready, z_diag, w3_zero, w3_moved = (
        m.sem(x) for x in ("power_ready", "ba_ready", "ca_ready", "z_ready", "z_diag", "w3_zero", "w3_moved"))
    root_ready, sq_ready = m.sem("root_ready"), m.sem("sq_ready")
    psteps, adummy, w1_ready = m.sem("psteps"), m.sem("adummy"), m.sem("w1_ready")

    FA, FC = 0, 1
    half0 = [2, 2 + 10]
    fm = lambda h: half0[h]
    fu = lambda h, jp: half0[h] + 1 + jp
    ft = lambda h, q: half0[h] + 5 + q
    ftm = lambda h: half0[h] + 9
    FW1 = 22
    FZ = FW1 + 8
    ring = m.ring(m.banks, ["act"] * (FZ + 8))
    for h in range(2):
        m.section_end[f"u{h}"] = (ring.filled, fu(h, TC // 2 - 1) + 1)

    with nc.Block() as block:
        @block.sync
        def _(sp):
            sp.dma_start(arow[:, 0, :], a["ev_a_re"][0].rearrange("(g e) n -> g (e n)", e=2)).then_inc(param_loaded, 16)
            sp.dma_start(arow[:, 1, :], a["ev_a_im"][0].rearrange("(g e) n -> g (e n)", e=2)).then_inc(param_loaded, 16)
            sp.dma_start(ldt, a["ev_log_dt"][0].rearrange("(g e) -> g e", e=2)).then_inc(param_loaded, 16)
            for r, name in enumerate(("ev_b_re", "ev_b_im")):
                for e in range(2):
                    sp.dma_start(braw[NST * e:NST * e + NST, r],
                                 a[name][0].rearrange("(g e) n c -> e n g c", e=2)[e]).then_inc(b_loaded, 16)
            for r, name in enumerate(("ev_c_re", "ev_c_im")):
                c = a[name][0].rearrange("(t g e) c n -> t g c e n", t=2, e=2)
                for t in range(2):
                    for g in range(G2 // 2):
                        sp.dma_start(craw[GC * g:GC * g + GC, r, t].rearrange("p (e n) -> p e n", e=2),
                                     c[t, g]).then_inc(c_loaded, 16)
            sp.dma_start(dcol, a["ev_d"][0].rearrange("g c -> c g")).then_inc(d_loaded, 16)
            for h in range(2):
                sp.wait_ge(um_evac, h + 1)
                for c in range(MCH):
                    for j in range(TC):
                        sp.dma_start(um2[c:c + 1, :, j], um16[TC * c + j:TC * c + j + 1, :]
                                     .rearrange("p (g c) -> p g c", c=GC)).then_inc(um_moved, 16)
            send_sections(m, sp, 3)
            sp.wait_ge(z_diag, 1)
            sp.wait_ge(w3_zero, 1)
            for j in range(TC):
                sp.dma_start(m.w3[GC * j:GC * j + GC, :, GC * j:P], zt[:, :, 0:P - GC * j]).then_inc(w3_moved, 16)
            sp.wait_ge(w3_moved, 16 * TC)

        @block.tensor
        def _(pe):
            def t_group(fill, dsts):
                ring.wait_free(pe, fill)
                for dst, src, ident in dsts:
                    last = nc.tensor.transpose(dst, src, ident)
                last.then_inc(ring.filled, 1)

            pe.wait_ge(arow_ready, 1)
            t_group(FA, [(ring.bank(FA)[:, G2 * i:G2 * i + G2], arow[:, i, :], m.ident[0:G2, 0:G2]) for i in range(3)])
            pe.wait_ge(c_loaded, 16 * 2 * G2)
            t_group(FC, [(ring.bank(FC)[:, P * (2 * r + t):P * (2 * r + t) + P], craw[:, r, t], m.ident[:, :])
                         for r in range(2) for t in range(2)])
            for h in range(2):
                w = section(m, f"u{h}")
                wait_section(m, pe, f"u{h}")
                ring.wait_free(pe, fm(h))
                row_product(nc, m, pe, ring.bank(fm(h))[0:META, 0:SEC], slice(0, META), w, 0, SEC).then_inc(ring.filled, 1)
                for jp in range(TC // 2):
                    ring.wait_free(pe, fu(h, jp))
                    for e in range(2):
                        j = 2 * jp + e
                        last = row_product(nc, m, pe, ring.bank(fu(h, jp))[:, e * SEC:e * SEC + SEC],
                                           slice(META + j, L, TC), w, 0, SEC)
                    last.then_inc(ring.filled, 1)
                pe.wait_ge(ring.emptied["act"], fu(h, 3) + 1)
                for q in range(4):
                    t_group(ft(h, q), [(ring.bank(ft(h, q))[:, P * i:P * i + P],
                                        m.urow[:, 4 * q + i], m.ident[:, :])
                                       for i in range(4)])
                pe.wait_ge(um_moved, 16 * META * (h + 1))
                t_group(ftm(h), [(ring.bank(ftm(h))[:, MCH * g:MCH * g + MCH], um2[:, g],
                                  m.ident[0:MCH, 0:MCH]) for g in range(16)])
            pe.wait_ge(ba_ready, 1)
            for q in range(8):
                t_group(FW1 + q, [(ring.bank(FW1 + q)[:, P * (2 * i + r):P * (2 * i + r) + P],
                                   m.ba[:, r, 2 * q + i], m.ident[:, :]) for i in range(2) for r in range(2)])
            pe.wait_ge(ca_ready, 1)
            for q in range(8):
                ring.wait_free(pe, FZ + q)
                for i in range(4):
                    g = 8 * (q // 2) + 2 * i + q % 2
                    rows = slice(NST * (g % 2), NST * (g % 2) + NST)
                    for r in range(2):
                        last = nc.tensor.matmul(ring.bank(FZ + q)[0:GC, P * i:P * i + P], m.ba[rows, r, g // 2, TC - 1],
                                                m.ca[rows, r, g // 2, 0:TC], start=(r == 0), stop=(r == 1))
                last.then_inc(ring.filled, 1)

        @block.scalar
        def _(act):
            def copy(dst, src, s, n=1):
                return act.activation(dst, src, ACT.Copy).then_inc(s, n)
            ring.wait_filled(act, FA)
            act.activation(dt, ring.bank(FA)[:, 2 * G2:3 * G2], ACT.Exp).then_inc(dt_ready, 1)
            act.activation(ai, ring.bank(FA)[:, G2:2 * G2], ACT.Copy).then_inc(dt_ready, 1)
            act.activation(ar, ring.bank(FA)[:, 0:G2], ACT.Copy).then_inc(dt_ready, 1)
            act.wait_ge(dt_ready, 3)
            act.nop().then_inc(ring.emptied["act"], 1)
            ring.wait_filled(act, FC)
            act.activation(m.ca[:, 0, :, 0], ring.bank(FC)[:, 0:256].rearrange("p (g c) -> p g c", g=G2),
                           ACT.Copy).then_inc(adummy, 1)
            act.activation(m.ca[:, 1, :, 0], ring.bank(FC)[:, 256:512].rearrange("p (g c) -> p g c", g=G2),
                           ACT.Copy, scale=-1.0).then_inc(adummy, 1)
            act.wait_ge(adummy, 2)
            act.nop().then_inc(ring.emptied["act"], 1)
            for h in range(2):
                ring.wait_filled(act, fm(h))
                if h:
                    act.wait_ge(um_moved, 16 * META * h)
                act.activation(um16, ring.bank(fm(h))[0:META, 0:SEC], ACT.Copy).then_inc(um_evac, 1)
                act.wait_ge(um_evac, h + 1)
                act.nop().then_inc(ring.emptied["act"], 1)
                for jp in range(TC // 2):
                    ring.wait_filled(act, fu(h, jp))
                    copy(m.urow[:, :, 2 * jp:2 * jp + 2].rearrange("p g j c -> p j g c"),
                         ring.bank(fu(h, jp)).rearrange("p (j g c) -> p j g c", j=2, c=GC),
                         ring.emptied["act"])
                for q in range(4):
                    g = 16 * h + 4 * q
                    ring.wait_filled(act, ft(h, q))
                    copy(m.uj[:, g:g + 4, MCH:NCH], ring.bank(ft(h, q)).rearrange("p (g c) -> p g c", g=4),
                         ring.emptied["act"])
                ring.wait_filled(act, ftm(h))
                copy(m.uj[:, 16 * h:16 * h + 16, 0:MCH],
                     ring.bank(ftm(h))[:, 0:16 * MCH].rearrange("p (g c) -> p g c", g=16), ring.emptied["act"])
                if h == 0:
                    act.wait_ge(sq_ready, 1)
                    act.activation(m.radius, s1, ACT.Sqrt).then_inc(root_ready, 1)
            for q in range(8):
                ring.wait_filled(act, FW1 + q)
                copy(m.w1[:, 2 * q:2 * q + 2], ring.bank(FW1 + q).rearrange("p (g r s) -> p g r s", g=2, r=2),
                     ring.emptied["act"])
            for q in range(8):
                ring.wait_filled(act, FZ + q)
                copy(zt[:, 8 * (q // 2):8 * (q // 2) + 8, :].rearrange("p (i e) n -> p i e n", e=2)[:, :, q % 2], ring.bank(FZ + q)[0:GC, :].rearrange("p (g n) -> p g n", g=4),
                     ring.emptied["act"])

        @block.vector
        def _(dve):
            c = Chain(dve, steps)

            def tt(o, x, y, op):
                return dve.tensor_tensor(o, x, y, op)

            def cmul(ore, oim, xr, xi, yr, yi, t):
                tt(t[0], xr, yr, ALU.mult)
                tt(t[1], xi, yi, ALU.mult)
                tt(t[2], xr, yi, ALU.mult)
                c.link(tt(t[3], xi, yr, ALU.mult))
                tt(ore, t[0], t[1], ALU.subtract)
                c.link(tt(oim, t[2], t[3], ALU.add))

            dve.wait_ge(param_loaded, 48)
            dve.tensor_copy(arow[:, 2, :].rearrange("p (e n) -> p e n", e=2), bc(ldt, 2, NST)).then_inc(arow_ready, 1)
            dve.wait_ge(dt_ready, 3)
            c.link(dve.tensor_scalar(ar, ar, -1e-4, None, ALU.min))
            f = 2.0 ** -LOG_SCALE
            dve.scalar_tensor_tensor(zr, ar, f, dt, ALU.mult, ALU.mult)
            c.link(dve.scalar_tensor_tensor(zi, ai, f, dt, ALU.mult, ALU.mult))
            c.link(dve.tensor_scalar(er, zr, 1.0 / TAYLOR, 1.0, ALU.mult, ALU.add))
            c.link(dve.tensor_scalar(ei, zi, 1.0 / TAYLOR, None, ALU.mult))
            for d in range(TAYLOR - 1, 1, -1):
                cmul(s1, s2, zr, zi, er, ei, (s3, s4, s5, m.msq[:, 0:G2]))
                dve.tensor_scalar(er, s1, 1.0 / d, 1.0, ALU.mult, ALU.add)
                c.link(dve.tensor_scalar(ei, s2, 1.0 / d, None, ALU.mult))
            cmul(s1, s2, zr, zi, er, ei, (s3, s4, s5, m.msq[:, 0:G2]))
            cur, nxt = (s1, s2), (er, ei)
            for _ in range(LOG_SCALE):
                (xr, xi), (yr, yi) = cur, nxt
                dve.scalar_tensor_tensor(s3, xr, 2.0, xr, ALU.add, ALU.mult)
                tt(s4, xi, xi, ALU.mult)
                c.link(dve.scalar_tensor_tensor(s5, xr, 1.0, xi, ALU.add, ALU.mult))
                tt(yr, s3, s4, ALU.subtract)
                c.link(dve.tensor_scalar(yi, s5, 2.0, None, ALU.mult))
                cur, nxt = nxt, cur
            xr, xi = cur
            s6, s7 = nxt
            dve.memset(pw[:, 0, 0], 1.0)
            dve.memset(pw[:, 0, 1], 0.0)
            dve.tensor_scalar(pw[:, 1, 0], xr, 1.0, None, ALU.add)
            c.link(dve.tensor_copy(pw[:, 1, 1], xi))
            tmps = [t[:, 0:4 * G2].rearrange("p (k g) -> p k g", g=G2) for t in t4]
            for n in (1, 2, 4):
                cmul(pw[:, n + 1:2 * n + 1, 0], pw[:, n + 1:2 * n + 1, 1], pw[:, 1:n + 1, 0], pw[:, 1:n + 1, 1],
                     bc(pw[:, n, 0], 1, n), bc(pw[:, n, 1], 1, n), [t[:, 0:n] for t in tmps])
            dve.nop().then_inc(power_ready, 1)
            tt(s3, ar, ar, ALU.mult)
            c.link(tt(s4, ai, ai, ALU.mult))
            c.link(tt(s3, s3, s4, ALU.add))
            c.link(dve.reciprocal(s3, s3))
            tt(s4, xr, ar, ALU.mult)
            tt(s5, xi, ai, ALU.mult)
            tt(s6, xi, ar, ALU.mult)
            c.link(tt(s7, xr, ai, ALU.mult))
            tt(s4, s4, s5, ALU.add)
            c.link(tt(s6, s6, s7, ALU.subtract))
            tt(zr, s4, s3, ALU.mult)
            c.link(tt(zi, s6, s3, ALU.mult))
            a8r, a8i = pw[:, TC, 0], pw[:, TC, 1]
            tt(s2, a8r, a8r, ALU.mult)
            c.link(tt(s3, a8i, a8i, ALU.mult))
            c.link(tt(s2, s2, s3, ALU.add))
            dve.tensor_scalar(s1, s2, 1e-30, None, ALU.max).then_inc(sq_ready, 1)
            dve.wait_ge(root_ready, 1)
            c.link(dve.reciprocal(s3, m.radius))
            c.link(tt(s3, s3, s1, ALU.mult))
            c.link(tt(s3, s3, m.radius, ALU.add))
            c.link(dve.tensor_scalar(m.radius, s3, 0.5, None, ALU.mult))
            c.link(dve.reciprocal(s3, m.radius))
            dve.memset(m.turn[:, 0, :, 0], 1.0)
            dve.memset(m.turn[:, 1, :, 0], 0.0)
            tt(m.turn[:, 0, :, 1], a8r, s3, ALU.mult)
            c.link(tt(m.turn[:, 1, :, 1], a8i, s3, ALU.mult))
            n = 1
            while n + 1 < NCH:
                k = min(n, NCH - 1 - n)
                tv = [t[:, 0:G2 * k].rearrange("p (g c) -> p g c", g=G2) for t in t4]
                cmul(m.turn[:, 0, :, n + 1:n + 1 + k], m.turn[:, 1, :, n + 1:n + 1 + k],
                     m.turn[:, 0, :, 1:1 + k], m.turn[:, 1, :, 1:1 + k],
                     bc(m.turn[:, 0, :, n], 2, k), bc(m.turn[:, 1, :, n], 2, k), tv)
                n += k
            dve.wait_ge(b_loaded, 64)
            bb = [m.ba[:, r, :, TC - 1] for r in range(2)]
            tv = [t[:, 0:G2 * GC].rearrange("p (g c) -> p g c", g=G2) for t in t4]
            cmul(bb[0], bb[1], bc(zr, 2, GC), bc(zi, 2, GC), braw[:, 0], braw[:, 1], tv)
            for j in range(TC - 1):
                cmul(m.ba[:, 0, :, j], m.ba[:, 1, :, j], bc(pw[:, TC - 1 - j, 0], 2, GC), bc(pw[:, TC - 1 - j, 1], 2, GC),
                     bb[0], bb[1], tv)
            dve.nop().then_inc(ba_ready, 1)
            dve.wait_ge(d_loaded, 16)
            dve.wait_ge(ring.emptied["act"], FZ + 8)
            diag = m.tmp[0:GC, 0:G * GC].rearrange("p (g c) -> p g c", g=G)
            c.link(tt(diag, bc(m.ident[0:GC, 0:GC], 1, G), bc(dcol, 2, GC), ALU.mult))
            tt(zt[:, :, 0:GC], zt[:, :, 0:GC], diag, ALU.add).then_inc(z_diag, 1)

        @block.gpsimd
        def _(pool):
            c = Chain(pool, psteps)
            pool.wait_ge(power_ready, 1)
            pool.wait_ge(ring.emptied["act"], 2)
            cr, ci = m.ca[:, 0, :, 0], m.ca[:, 1, :, 0]
            tv = [t[:, 0:G2 * GC].rearrange("p (g c) -> p g c", g=G2) for t in pt]
            for k in range(1, TC + 1):
                pr, pi = bc(pw[:, k, 0], 2, GC), bc(pw[:, k, 1], 2, GC)
                pool.tensor_tensor(tv[0], cr, pr, ALU.mult)
                pool.tensor_tensor(tv[1], ci, pi, ALU.mult)
                pool.tensor_tensor(tv[2], ci, pr, ALU.mult)
                c.link(pool.tensor_tensor(tv[3], cr, pi, ALU.mult))
                pool.tensor_tensor(m.ca[:, 0, :, k], tv[0], tv[1], ALU.add)
                c.link(pool.tensor_tensor(m.ca[:, 1, :, k], tv[2], tv[3], ALU.subtract))
            pool.nop().then_inc(ca_ready, 1)
            pool.wait_ge(ring.emptied["act"], ftm(1) + 1)
            pool.memset(m.w3, 0.0).then_inc(w3_zero, 1)


def s5_stage(nc, m, a):
    yq = [m.urow.rearrange("p g j c -> p (g j c)")[:, 1024 * i:1024 * (i + 1)].rearrange("p (j n) -> p j n", j=TC)
          for i in range(2)]
    ymall = m.tmp[0:MCH, 0:1024].rearrange("p (j n) -> p j n", j=TC)
    w1flat = m.w1.rearrange("p g r s -> p (g r s)")
    ym = [w1flat[0:MCH, 1024 + 1024 * i:2048 + 1024 * i].rearrange("p (j n) -> p j n", j=TC) for i in range(2)]
    sg = [w1flat[:, 400 * i:400 * i + 400] for i in range(2)]
    tm = [m.tmp[:, 1008 * i:1008 * i + 910] for i in range(2)]

    by, index = [], {}

    def plan(key, who):
        index[key] = len(by)
        by.append(who)

    for g in range(G2):
        plan(("v", g), "act")
    gates = [("gs", 4), ("gb", 0)]
    for name, base in gates:
        for mt in range(4):
            for ch in range(3):
                plan(("gate", base + mt, ch), "act")

    def y_fills(kk):
        for q in range(2):
            plan(("y", kk, q), "act")
            plan(("ym", kk, q), "act")

    def t_fills(kk):
        for q in range(3):
            plan(("t", kk, q), "dve")

    order = [("y", 0), ("y", 1), ("t", 0), ("y", 2), ("t", 1), ("y", 3), ("t", 2), ("t", 3)]
    for what, kk in order:
        (y_fills if what == "y" else t_fills)(kk)
    for mt in range(4):
        for ch in range(3):
            plan(("glu", mt, ch), "act")
    ring = m.ring(m.banks, by)
    for name, base in gates:
        for half in range(2):
            m.section_end[f"{name}{half}"] = (ring.filled, index[("gate", base + 2 * half + 1, 2)] + 1)
    m.section_end["glu"] = (ring.filled, len(by))
    steps, states_ready, sg_used, glu_done, w1_free = (m.sem(x) for x in ("steps", "states_ready", "sg_used", "glu_done", "w1_free"))
    acount = lambda n: by[:n + 1].count("act")
    dcount = lambda n: by[:n + 1].count("dve")

    with nc.Block() as block:
        @block.sync
        def _(sp):
            send_sections(m, sp, m.section_at["q1"])

        @block.tensor
        def _(pe):
            def fill(key):
                n = index[key]
                ring.wait_free(pe, n)
                return ring.bank(n)

            for g2 in range(G2):
                b = fill(("v", g2))
                for e in range(2):
                    for r in range(2):
                        last = nc.tensor.matmul(b[NST * e:NST * e + NST, NCH * r:NCH * r + NCH],
                                                m.w1[:, g2, r, NST * e:NST * e + NST], m.uj[:, 2 * g2 + e, :],
                                                start=True, stop=True)
                last.then_inc(ring.filled, 1)
            for name, base in gates:
                for mt in range(4):
                    sec = f"{name}{mt // 2}"
                    w = section(m, sec)
                    if mt % 2 == 0:
                        wait_section(m, pe, sec)
                    for ch, (c0, c1) in enumerate(CHUNKS):
                        b = fill(("gate", base + mt, ch))
                        col_product(nc, m, pe, b[:, 0:c1 - c0],
                                    lambda k: w[:, k, P * (mt % 2):P * (mt % 2) + P],
                                    lambda k: m.xnT[:, k, c0:c1]).then_inc(ring.filled, 1)
            pe.wait_ge(states_ready, 1)
            for what, kk in order:
                if what == "y":
                    for q in range(2):
                        for meta in range(2):
                            b = fill(("ym" if meta else "y", kk, q))
                            cols = slice(0, MCH) if meta else slice(MCH, NCH)
                            n = MCH if meta else P
                            for i in range(4):
                                g = 8 * kk + 2 * i + q
                                rows = slice(NST * (g % 2), NST * (g % 2) + NST)
                                dst = b[0:n, P * i:P * i + P]
                                for r in range(2):
                                    nc.tensor.matmul(dst, m.v[rows, r, g // 2, cols], m.ca[rows, r, g // 2, 1:TC + 1],
                                                     start=(r == 0), stop=False)
                                last = nc.tensor.matmul(dst, m.uj[:, g, cols], m.w3[:, g, :], start=False, stop=True)
                            last.then_inc(ring.filled, 1)
                else:
                    n = index[("ym", kk, 1)]
                    pe.wait_ge(ring.emptied["act"], acount(n))
                    for q in range(2):
                        b = fill(("t", kk, q))
                        for i in range(4):
                            last = nc.tensor.transpose(b[:, P * i:P * i + P], yq[kk % 2][:, 4 * q + i, :], m.ident[:, :])
                        last.then_inc(ring.filled, 1)
                    b = fill(("t", kk, 2))
                    for j in range(TC):
                        last = nc.tensor.transpose(b[:, MCH * j:MCH * j + MCH], ym[kk % 2][:, j, :], m.ident[0:MCH, 0:MCH])
                    last.then_inc(ring.filled, 1)
            wait_section(m, pe, "glu")
            w = section(m, "glu")
            pe.wait_ge(ring.emptied["dve"], dcount(index[("t", 3, 2)]))
            for mt in range(4):
                for ch, (c0, c1) in enumerate(CHUNKS):
                    b = fill(("glu", mt, ch))
                    col_product(nc, m, pe, b[:, 0:c1 - c0], lambda k: w[:, k, P * mt:P * mt + P],
                                lambda k: m.yT[:, k, c0:c1], 4).then_inc(ring.filled, 1)

        @block.scalar
        def _(act):
            done = ring.emptied["act"]
            for g2 in range(G2):
                n = index[("v", g2)]
                ring.wait_filled(act, n)
                act.activation(m.v[:, :, g2, 1:NCH + 1], ring.bank(n)[:, 0:2 * NCH].rearrange("p (r c) -> p r c", r=2),
                               ACT.Copy).then_inc(done, 1)
            for name, base in gates:
                for mt in range(4):
                    for ch, (c0, c1) in enumerate(CHUNKS):
                        n = index[("gate", base + mt, ch)]
                        ring.wait_filled(act, n)
                        act.activation(m.mixT[:, base + mt, c0:c1], ring.bank(n)[:, 0:c1 - c0], ACT.Silu).then_inc(done, 1)
            for what, kk in order:
                if what != "y":
                    continue
                if kk >= 2:
                    act.wait_ge(ring.filled, index[("t", kk - 2, 2)] + 1)
                for q in range(2):
                    for key, dst, rows in (("y", yq, P), ("ym", ym, MCH)):
                        n = index[(key, kk, q)]
                        ring.wait_filled(act, n)
                        o = dst[kk % 2].rearrange("p j (g e c) -> p e g j c", e=2, c=GC)[:, q]
                        act.activation(o, ring.bank(n)[0:rows, :].rearrange("p (g j c) -> p g j c", g=4, j=TC),
                                       ACT.Gelu_apprx_tanh).then_inc(done, 1)
            i = 0
            for mt in range(4):
                for ch, (c0, c1) in enumerate(CHUNKS):
                    n = index[("glu", mt, ch)]
                    ring.wait_filled(act, n)
                    if i >= 2:
                        act.wait_ge(sg_used, i - 1)
                    act.activation(sg[i % 2][:, 0:c1 - c0], ring.bank(n)[:, 0:c1 - c0], ACT.Sigmoid,
                                   bias=m.bglu[:, mt:mt + 1]).then_inc(done, 1)
                    i += 1

        @block.vector
        def _(dve):
            c = Chain(dve, steps)
            H = G2 // 2 - 1

            def tt(o, x, y, op):
                return dve.tensor_tensor(o, x, y, op)

            c.link(dve.memset(m.v[:, :, :, 0], 0.0))
            parts = [(0, 7), (7, 14), (14, 16)]
            for g0, g1 in parts:
                n = g1 - g0
                dve.wait_ge(ring.emptied["act"], acount(index[("v", g1 - 1)]))
                vr, vi = m.v[:, 0, g0:g1, 1:NCH + 1], m.v[:, 1, g0:g1, 1:NCH + 1]
                pr, pi = m.turn[:, 0, g0:g1, :], m.turn[:, 1, g0:g1, :]
                t0, t1 = (t[:, 0:n * NCH].rearrange("p (g c) -> p g c", g=n) for t in tm)
                tt(t0, vr, pr, ALU.mult)
                c.link(tt(t1, vr, pi, ALU.mult))
                tt(vr, vi, pi, ALU.mult)
                c.link(tt(vi, vi, pr, ALU.mult))
                tt(vr, vr, t0, ALU.add)
                c.link(tt(vi, vi, t1, ALU.subtract))
                for g in range(g0, g1):
                    for r in range(2):
                        row = m.v[:, r, g, 1:NCH + 1]
                        ins = dve.tensor_tensor_scan(row, m.radius[:, g:g + 1].broadcast_to((P, NCH)), row, 0.0,
                                                     ALU.mult, ALU.add)
                c.link(ins)
                tt(t0, vr, pr, ALU.mult)
                c.link(tt(t1, vr, pi, ALU.mult))
                tt(vr, vi, pi, ALU.mult)
                c.link(tt(vi, vi, pr, ALU.mult))
                dve.tensor_tensor(vr, t0, vr, ALU.subtract)
                c.link(tt(vi, vi, t1, ALU.add))
            dve.nop().then_inc(states_ready, 1)
            for kk in range(4):
                frames = m.yT[:, kk, META:L].rearrange("p (c j) -> p j c", j=TC)
                for q in range(2):
                    n = index[("t", kk, q)]
                    ring.wait_filled(dve, n)
                    dve.tensor_copy(frames[:, 4 * q:4 * q + 4], ring.bank(n).rearrange("p (j c) -> p j c", j=4)
                                    ).then_inc(ring.emptied["dve"], 1)
                n = index[("t", kk, 2)]
                ring.wait_filled(dve, n)
                dve.tensor_copy(m.yT[:, kk, 0:META].rearrange("p (c j) -> p j c", j=TC),
                                ring.bank(n)[:, 0:META].rearrange("p (j c) -> p j c", j=TC)
                                ).then_inc(ring.emptied["dve"], 1)
            dve.wait_ge(ring.emptied["dve"], by.count("dve"))
            i = 0
            for mt in range(4):
                for ch, (c0, c1) in enumerate(CHUNKS):
                    dve.wait_ge(ring.emptied["act"], acount(index[("glu", mt, ch)]))
                    s = sg[i % 2][:, 0:c1 - c0]
                    c.link(tt(s, s, m.yT[:, mt, c0:c1], ALU.mult))
                    g = m.mixT[:, 4 + mt, c0:c1]
                    tt(g, g, s, ALU.mult).then_inc(sg_used, 1)
                    i += 1


def feature_stage(nc, m, area, tiles, sources, upto):
    zt = [area.take(f"z{i}_{upto}", L) for i in range(2)]
    sq = [area.take(f"squares{i}_{upto}", L) for i in range(2)]
    rs = area.take(f"root_{upto}", L)
    NM = len(tiles)
    by, index = [], {}

    def plan(key, who):
        index[key] = len(by)
        by.append(who)

    for i in range(NM + 2):
        if i < NM:
            for c in range(len(tiles[i]["chunks"])):
                plan(("mm", i, c), "act")
        if 0 <= i - 1 < NM:
            t = tiles[i - 1]
            if t["kind"] == "n":
                for c in range(len(t["chunks"])):
                    plan(("ms", i - 1, c), "act")
            elif t["kind"] == "r":
                for c in range(3):
                    plan(("tr", i - 1, c), "dve")
        if 0 <= i - 2 < NM and "dup" in tiles[i - 2]:
            for v in range(2):
                for c in range(3):
                    plan(("dup", i - 2, v, c), "dve")
    ring = m.ring(m.banks, by)
    normal = [i for i in range(NM) if tiles[i]["kind"] == "n"]
    w_hi, w_lo, w_first_hi, w_first, squared, copied, rooted, inverted, finished = (
        m.sem(x) for x in ("w_hi", "w_lo", "w_first_hi", "w_first", "squared", "copied", "rooted", "inverted", "finished"))
    xs = [m.sem(x) for x in ("x_hi_act", "x_hi_dve", "x_lo_pool", "x_lo_dve")]
    for i, t in enumerate(tiles):
        m.section_end[t["section"]] = (w_lo, i) if i >= 2 else (ring.filled, index[("mm", i, 2)] + 1)
    acount = lambda n: by[:n + 1].count("act")

    def raw_weights(i):
        t = tiles[i]
        return section(m, t["section"])[:, :, P * t["half"]:P * t["half"] + P]

    with nc.Block() as block:
        @block.sync
        def _(sp):
            send_sections(m, sp, upto)

        @block.tensor
        def _(pe):
            for i in range(NM + 2):
                if i < NM:
                    t = tiles[i]
                    if i == 0:
                        pe.wait_ge(w_first, 1)
                    else:
                        pe.wait_ge(w_lo, i)
                    for c, (c0, c1) in enumerate(t["chunks"]):
                        n = index[("mm", i, c)]
                        ring.wait_free(pe, n)
                        before = (lambda k: wait_split(pe, k, xs)) if (i == 0 and c == 0) else None
                        split_product(nc, ring.bank(n)[:, 0:c1 - c0], lambda k: (m.whi[i % 2][:, k], m.wlo[i % 2][:, k]),
                                      lambda k: (m.xhi[:, k, c0:c1], m.xlo[:, k, c0:c1]), before=before
                                      ).then_inc(ring.filled, 1)
                if 0 <= i - 1 < NM:
                    t = tiles[i - 1]
                    if t["kind"] == "n":
                        for c, (c0, c1) in enumerate(t["chunks"]):
                            n = index[("ms", i - 1, c)]
                            ring.wait_free(pe, n)
                            pe.wait_ge(ring.emptied["act"], acount(index[("mm", i - 1, c)]))
                            nc.tensor.matmul(ring.bank(n)[:, 0:c1 - c0], m.headmean[:, :], sq[(i - 1) % 2][:, c0:c1],
                                             start=True, stop=True).then_inc(ring.filled, 1)
                    elif t["kind"] == "r":
                        pe.wait_ge(ring.emptied["act"], acount(index[("mm", i - 1, 2)]))
                        z = zt[(i - 1) % 2]
                        for c in range(3):
                            n = index[("tr", i - 1, c)]
                            ring.wait_free(pe, n)
                            if c == 2:
                                last = nc.tensor.transpose(ring.bank(n)[0:META, 0:P], z[:, 0:META], m.ident[:, :])
                            else:
                                for b in range(4):
                                    c0 = META + P * (4 * c + b)
                                    last = nc.tensor.transpose(ring.bank(n)[:, P * b:P * b + P], z[:, c0:c0 + P], m.ident[:, :])
                            last.then_inc(ring.filled, 1)
                if 0 <= i - 2 < NM and "dup" in tiles[i - 2]:
                    t = tiles[i - 2]
                    pe.wait_ge(finished, normal.index(i - 2) + 1)
                    for v in range(2):
                        for c, (c0, c1) in enumerate(CHUNKS):
                            n = index[("dup", i - 2, v, c)]
                            ring.wait_free(pe, n)
                            nc.tensor.matmul(ring.bank(n)[:, 0:c1 - c0], m.kvcopy[:, P * v:P * v + P], t["dst"](c0, c1),
                                             start=True, stop=True).then_inc(ring.filled, 1)

        @block.scalar
        def _(act):
            split_tiles(act, None, None, sources, m.xhi, m.xlo, ON_ACT, xs)

            def round_weights(i):
                if i == 0 or i >= NM:
                    return
                if i >= 2:
                    act.wait_ge(ring.filled, index[("mm", i - 2, len(tiles[i - 2]["chunks"]) - 1)] + 1)
                wait_section(m, act, tiles[i]["section"])
                act.activation(m.whi[i % 2], raw_weights(i), ACT.Copy).then_inc(w_hi, 1)

            for i in range(NM + 1):
                if i < NM:
                    t = tiles[i]
                    round_weights(i + 1)
                    if t["kind"] in "nr" and i >= 2:
                        p = tiles[i - 2]
                        if p["kind"] == "n":
                            act.wait_ge(finished, normal.index(i - 2) + 1)
                        elif p["kind"] == "r":
                            act.wait_ge(ring.filled, index[("tr", i - 2, 2)] + 1)
                    for c, (c0, c1) in enumerate(t["chunks"]):
                        n = index[("mm", i, c)]
                        ring.wait_filled(act, n)
                        z = ring.bank(n)[:, 0:c1 - c0]
                        if t["kind"] == "n":
                            act.activation(zt[i % 2][:, c0:c1], z, ACT.Copy).then_inc(copied, 1)
                            act.activation(sq[i % 2][:, c0:c1], z, ACT.Square).then_inc(ring.emptied["act"], 1)
                        elif t["kind"] == "r":
                            act.activation(zt[i % 2][:, c0:c1], z, ACT.Copy).then_inc(ring.emptied["act"], 1)
                        else:
                            act.activation(t["dst"](c0, c1), z, ACT.Silu if t["kind"] == "g" else ACT.Copy
                                           ).then_inc(ring.emptied["act"], 1)
                if 0 <= i - 1 and tiles[i - 1]["kind"] == "n":
                    k = normal.index(i - 1)
                    if k >= 1:
                        act.wait_ge(finished, k)
                    for c, (c0, c1) in enumerate(tiles[i - 1]["chunks"]):
                        n = index[("ms", i - 1, c)]
                        ring.wait_filled(act, n)
                        act.activation(rs[:, c0:c1], ring.bank(n)[:, 0:c1 - c0], ACT.Sqrt, bias=m.eps
                                       ).then_inc(ring.emptied["act"], 1)

        @block.gpsimd
        def _(pool):
            split_tiles(None, None, pool, sources, m.xhi, m.xlo, ON_ACT, xs)
            for i in range(1, NM):
                pool.wait_ge(w_hi, i)
                if i >= 2:
                    pool.wait_ge(ring.filled, index[("mm", i - 2, len(tiles[i - 2]["chunks"]) - 1)] + 1)
                pool.tensor_tensor(m.wlo[i % 2], raw_weights(i), m.whi[i % 2].bitcast(F32), ALU.subtract).then_inc(w_lo, 1)

        @block.vector
        def _(dve):
            wait_section(m, dve, tiles[0]["section"])
            dve.tensor_copy(m.whi[0], raw_weights(0)).then_inc(w_first_hi, 1)
            dve.wait_ge(w_first_hi, 1)
            dve.tensor_tensor(m.wlo[0], raw_weights(0), m.whi[0].bitcast(F32), ALU.subtract).then_inc(w_first, 1)
            split_tiles(None, dve, None, sources, m.xhi, m.xlo, ON_ACT, xs)
            for i in range(1, NM + 2):
                if 0 <= i - 1 < NM:
                    t = tiles[i - 1]
                    if t["kind"] == "n":
                        k = normal.index(i - 1)
                        c0, c1 = t["chunks"][0][0], t["chunks"][-1][1]
                        dve.wait_ge(ring.emptied["act"], acount(index[("ms", i - 1, len(t["chunks"]) - 1)]))
                        dve.reciprocal(rs[:, c0:c1], rs[:, c0:c1]).then_inc(inverted, 1)
                        dve.wait_ge(inverted, k + 1)
                        dve.scalar_tensor_tensor(t["dst"](c0, c1), zt[(i - 1) % 2][:, c0:c1], t["gain"], rs[:, c0:c1],
                                                 ALU.mult, ALU.mult).then_inc(finished, 1)
                    elif t["kind"] == "r":
                        for c in range(3):
                            n = index[("tr", i - 1, c)]
                            ring.wait_filled(dve, n)
                            if c == 2:
                                dst, src = t["rows"](0, 1)[0:META, 0], ring.bank(n)[0:META, 0:P]
                            else:
                                dst, src = t["rows"](1 + 4 * c, 5 + 4 * c), ring.bank(n).rearrange("p (t n) -> p t n", t=4)
                            dve.tensor_copy(dst, src).then_inc(ring.emptied["dve"], 1)
                if 0 <= i - 2 and "dup" in tiles[i - 2]:
                    for v in range(2):
                        for c, (c0, c1) in enumerate(CHUNKS):
                            n = index[("dup", i - 2, v, c)]
                            ring.wait_filled(dve, n)
                            dve.tensor_copy(tiles[i - 2]["dup"][:, v, c0:c1], ring.bank(n)[:, 0:c1 - c0]
                                            ).then_inc(ring.emptied["dve"], 1)


def qkv_stage(nc, m, a, area):
    m.qT = m.qk[:, 0:4 * L].rearrange("p (k l) -> p k l", k=4)
    m.kT = m.qk[:, 4 * L:8 * L].rearrange("p (k l) -> p k l", k=4)
    m.vrow = m.vrows.rearrange("p (t n) -> p t n", t=NT)
    tiles = []
    for side, dst in (("q", m.qT), ("k", m.kT)):
        for p in range(NPAIR):
            tiles.append(dict(kind="n", section=f"{side}{p // 2}", half=p % 2, chunks=CHUNKS, gain=m.head_gain["ev" + side],
                              dst=lambda c0, c1, d=dst, p=p: d[:, p, c0:c1]))
    for p in range(NPAIR):
        tiles.append(dict(kind="r", section=f"v{p // 2}", half=p % 2, chunks=CHUNKS,
                          rows=lambda t0, t1, p=p: m.vrow[:, t0:t1, P * p:P * p + P]))
    feature_stage(nc, m, area, tiles, m.xnT, m.section_at["eo1"])


def stick_breaking_stage(nc, m, a, area):
    def take(n, slots, name):
        return [area.take(f"{name}{i}", n).rearrange("p (h n) -> p h n", h=2) for i in range(slots)]

    W = 400
    lg = take(2 * W, 2, "log")
    sp_ = take(2 * W, 3, "softplus")
    wt = take(2 * W, 2, "weights")
    total = take(2 * W, 2, "total")

    its, finals = [], []
    for p in range(NPAIR):
        for ch, (c0, c1) in enumerate(CHUNKS):
            blocks = [b for b in range(NT) if tile_cols(b)[0] < c1]
            for b in reversed(blocks):
                k0, kn = tile_cols(b)
                q0 = max(c0, k0)
                its.append(dict(p=p, ch=ch, b=b, k0=k0, kn=kn, q0=q0, q1=c1, c0=c0, n=c1 - q0,
                                diag=k0 >= c0, first=b == blocks[-1], last=b == 0, acc=len(finals)))
            finals.append((p, ch, len(its) - 1))
    NI = len(its)
    z = [w[:, :].rearrange("p (h n) -> p h n", h=2) for w in m.wide]
    acc = [b[:, :] for b in m.bank]
    scored, capped, logged, softened, summed, weighted, weighed = (
        m.sem(x) for x in ("scored", "capped", "logged", "softened", "summed", "weighted", "weighed"))
    exped, totalled, finished, tsteps = m.sem("exped"), m.sem("totalled"), m.sem("finished"), m.sem("tsteps")

    with nc.Block() as block:
        @block.tensor
        def _(pe):
            def score(i):
                t = its[i]
                if i >= 3:
                    pe.wait_ge(weighted, i - 2)
                for h in range(2):
                    r = slice(HD * h, HD * h + HD)
                    dst = z[i % 3][0:t["kn"], h, 0:t["n"]]
                    last = nc.tensor.matmul(dst, m.kT[r, t["p"], t["k0"]:t["k0"] + t["kn"]], m.qT[r, t["p"], t["q0"]:t["q1"]],
                                            start=True, stop=not t["diag"])
                    if t["diag"]:
                        kn = t["kn"]
                        last = nc.tensor.matmul(z[i % 3][0:kn, h, 0:kn], m.identb[0:kn, 0:kn], m.negmask[0:kn, 0:kn],
                                                start=False, stop=True)
                last.then_inc(scored, 1)

            def take_sums(i):
                t = its[i]
                kn = t["kn"]
                pe.wait_ge(softened, i + 1)
                if not t["first"]:
                    pe.wait_ge(totalled, i)
                for h in range(2):
                    last = nc.tensor.matmul(z[i % 3][0:kn, h, 0:t["n"]], m.tri[0:kn, 0:kn], sp_[i % 3][0:kn, h, 0:t["n"]],
                                            start=False, stop=True, skip_group_check=True)
                    if not t["first"]:
                        o = its[i - 1]["q0"] - t["q0"]
                        q = its[i - 1]["q0"] - t["c0"]
                        last = nc.tensor.matmul(z[i % 3][0:kn, h, o:t["n"]], m.ones[:, 0:kn],
                                                total[(i - 1) % 2][:, h, q:t["q1"] - t["c0"]],
                                                start=False, stop=True, skip_group_check=True)
                last.then_inc(summed, 1)

            def weigh(i):
                t = its[i]
                pe.wait_ge(weighted, i + 1)
                if t["first"] and t["acc"] >= 2:
                    pe.wait_ge(finished, t["acc"] - 1)
                for h in range(2):
                    hh = 2 * t["p"] + h
                    last = nc.tensor.matmul(acc[t["acc"] % 2][HD * h:HD * h + HD, t["q0"] - t["c0"]:t["q1"] - t["c0"]],
                                            m.vrow[0:t["kn"], t["b"], HD * hh:HD * hh + HD], wt[i % 2][0:t["kn"], h, 0:t["n"]],
                                            start=t["first"], stop=t["last"], skip_group_check=True)
                last.then_inc(weighed, 1)

            for i in range(NI + 3):
                if 0 <= i - 2 < NI:
                    take_sums(i - 2)
                if i < NI:
                    score(i)
                if 0 <= i - 3 < NI:
                    weigh(i - 3)

        @block.scalar
        def _(act):
            act.preload_act_table_set("natural_log_exp_and_others")

            def weights(i):
                t = its[i]
                act.wait_ge(summed, i + 1)
                if i >= 2:
                    act.wait_ge(weighed, i - 1)
                act.activation(wt[i % 2][0:t["kn"], :, 0:t["n"]], z[i % 3][0:t["kn"], :, 0:t["n"]], ACT.Exp).then_inc(weighted, 1)

            for i in range(NI + 2):
                if 0 <= i - 2 < NI:
                    weights(i - 2)
                if i < NI:
                    t = its[i]
                    v = lg[i % 2][0:t["kn"], :, 0:t["n"]]
                    act.wait_ge(capped, i + 1)
                    act.activation(v, v, ACT.Exp, scale=-1.0).then_inc(exped, 1)
                    act.wait_ge(exped, i + 1)
                    act.activation(v, v, ACT.Ln, bias=1.0).then_inc(logged, 1)

        @block.vector
        def _(dve):
            ends = {last: n for n, (_, _, last) in enumerate(finals)}

            def finish(n):
                p, ch, last = finals[n]
                c0, c1 = CHUNKS[ch]
                dve.wait_ge(weighed, last + 1)
                g = m.mixT[:, p, c0:c1]
                dve.tensor_tensor(g, g, acc[n % 2][:, 0:c1 - c0], ALU.mult).then_inc(finished, 1)

            for i in range(NI + 4):
                if i < NI:
                    t = its[i]
                    zz = z[i % 3][0:t["kn"], :, 0:t["n"]]
                    v = lg[i % 2][0:t["kn"], :, 0:t["n"]]
                    dve.wait_ge(scored, i + 1)
                    if i >= 2:
                        dve.wait_ge(softened, i - 1)
                    dve.tensor_scalar(v.bitcast(I32), zz.bitcast(I32), 0x7FFFFFFF, None, ALU.bitwise_and).then_inc(capped, 1)
                    dve.wait_ge(logged, i + 1)
                    if i >= 3:
                        dve.wait_ge(summed, i - 2)
                        if i - 3 >= 0:
                            dve.wait_ge(totalled, i - 2)
                    dve.scalar_tensor_tensor(sp_[i % 3][0:t["kn"], :, 0:t["n"]], zz, 0.0, v, ALU.max, ALU.add).then_inc(softened, 1)
                if i - 4 in ends:
                    finish(ends[i - 4])

        @block.gpsimd
        def _(pool):
            for i in range(NI):
                t = its[i]
                pool.wait_ge(softened, i + 1)
                if i >= 2:
                    pool.wait_ge(summed, i)
                if i >= 1:
                    pool.wait_ge(totalled, i)
                q0, q1 = t["q0"] - t["c0"], t["q1"] - t["c0"]
                s, dst, src = sp_[i % 3], total[i % 2], total[(i - 1) % 2]
                if t["last"]:
                    pool.nop().then_inc(totalled, 1)
                elif t["first"]:
                    pool.tensor_copy(dst[:, :, q0:q1], s[:, :, 0:t["n"]]).then_inc(totalled, 1)
                else:
                    o = its[i - 1]["q0"] - t["c0"]
                    if o > q0:
                        pool.tensor_copy(dst[:, :, q0:o], s[:, :, 0:o - q0]).then_inc(tsteps, 1)
                    pool.tensor_tensor(dst[:, :, o:q1], src[:, :, o:q1], s[:, :, o - q0:t["n"]], ALU.add).then_inc(totalled, 1)


def split_mix(m, area, layer):
    src = m.mixT
    m.mlo = m.mixlo.rearrange("p (k l) -> p k l", k=KD)
    m.mhi = area.take(f"mix_hi{layer}", 8 * L, F32R).rearrange("p (k l) -> p k l", k=KD)
    return src


def out_weights(area, layer):
    return [[area.take(f"wo_{part}{layer}{i}", KD * SEC, F32R).rearrange("p (k n) -> p k n", k=KD) for i in range(2)]
            for part in ("hi", "lo")]


def out_split_engines(m, act, dve, pool, src, names, whi, wlo, xs, ws, free, first=0):
    w_hi, w_lo, w_first_hi, w_first = ws
    src, hi, lo = (x[:, :, first:L] for x in (src, m.mhi, m.mlo))
    if act:
        split_tiles(act, None, None, src, hi, lo, ON_ACT, xs)
    if dve:
        wait_section(m, dve, names[0])
        raw = section(m, names[0])
        dve.tensor_copy(whi[0], raw).then_inc(w_first_hi, 1)
        dve.wait_ge(w_first_hi, 1)
        dve.tensor_tensor(wlo[0], raw, whi[0].bitcast(F32), ALU.subtract).then_inc(w_first, 1)
        split_tiles(None, dve, None, src, hi, lo, ON_ACT, xs)
    if pool:
        split_tiles(None, None, pool, src, hi, lo, ON_ACT, xs)
    if act:
        for n in range(1, 4):
            if n >= 2:
                act.wait_ge(*free(n - 2))
            wait_section(m, act, names[n])
            act.activation(whi[n % 2], section(m, names[n]), ACT.Copy).then_inc(w_hi, 1)
    if pool:
        for n in range(1, 4):
            pool.wait_ge(w_hi, n)
            if n >= 2:
                pool.wait_ge(*free(n - 2))
            pool.tensor_tensor(wlo[n % 2], section(m, names[n]), whi[n % 2].bitcast(F32), ALU.subtract).then_inc(w_lo, 1)


def out_product(nc, m, pe, ring, i, cols, n, rows, whi, wlo, xs, ws, first):
    ring.wait_free(pe, i)
    before = (lambda k: wait_split(pe, k, xs)) if first else None
    split_product(nc, ring.bank(i)[0:rows, 0:SEC], lambda k: (m.mhi[:, k, cols], m.mlo[:, k, cols]),
                  lambda k: (whi[n % 2][:, k], wlo[n % 2][:, k]), before=before).then_inc(ring.filled, 1)


def wait_out_weights(pe, ws, n):
    if n == 0:
        pe.wait_ge(ws[3], 1)
    else:
        pe.wait_ge(ws[1], n)


def even_out_stage(nc, m, a, area):
    f = area.take("h1_rows", HEAD)
    m.xn = area.take("xn1", KD * L)
    m.xnT = m.xn.rearrange("p (k l) -> p k l", k=KD)
    src = split_mix(m, area, 0)
    whi, wlo = out_weights(area, 0)
    h1 = f[:, 0:NT * D].rearrange("p (t n) -> p t n", t=NT)
    xs_ = [f[:, NT * D + D * i:NT * D + D * (i + 1)] for i in range(2)]
    junk = f[:, NT * D + 2 * D:NT * D + 3 * D]
    m.h1_dram = nc.dram_tensor("h1_frames", (SEQ, D), F32, kind="Internal").ap()
    m.h1_stored = m.sem("h1_stored")
    row_loaded = [m.sem("row_loaded") for _ in range(3)]
    names = [f"eo{n}" for n in range(4)]
    by, index = [], {}

    def plan(key, who):
        index[key] = len(by)
        by.append(who)

    for n in range(3):
        for t in range(NT):
            plan(("mm", n, t), "dve")
    for t in range(NT + 2):
        if t < NT:
            plan(("mm", 3, t), "dve")
        if t >= 2:
            for h in range(2):
                plan(("tr", t - 2, h), "dve")
    ring = m.ring(m.banks, by)
    xs = [m.sem(x) for x in ("mix_hi_act", "mix_hi_dve", "mix_lo_pool", "mix_lo_dve")]
    ws = [m.sem(x) for x in ("w_hi", "w_lo", "w_first_hi", "w_first")]
    for n in range(4):
        m.section_end[names[n]] = (ws[1], n) if n else (ws[3], 1)
    free = lambda n: (ring.filled, index[("mm", n, NT - 1)] + 1)
    sq_done, ms_done, rt_done, rs_done, scaled = (m.sem(x) for x in ("sq_done", "ms_done", "rt_done", "rs_done", "scaled"))
    dcount = lambda n: by[:n + 1].count("dve")

    with nc.Block() as block:
        @block.sync
        def _(sp):
            sp.dma_start(h1[0:META, 0, :], a["meta_tokens"]).then_inc(row_loaded[0], 16)
            for h in range(2):
                sp.dma_start(h1[:, 1 + 4 * h:5 + 4 * h, :], a["x"][0, 512 * h:512 * h + 512, :]
                             .rearrange("(t p) n -> p t n", p=P)).then_inc(row_loaded[1 + h], 16)
            send_sections(m, sp, m.section_at["oq0"])
            for t in range(1, NT):
                sp.wait_ge(ring.emptied["dve"], dcount(index[("mm", 3, t)]))
                sp.dma_start(m.h1_dram[P * (t - 1):P * t, :], h1[:, t, :]).then_inc(m.h1_stored, 16)
            sp.wait_ge(m.h1_stored, 16 * (NT - 1))

        @block.tensor
        def _(pe):
            def product(n, t):
                c0, rows = tile_cols(t)
                if t == 0:
                    wait_out_weights(pe, ws, n)
                out_product(nc, m, pe, ring, index[("mm", n, t)], slice(c0, c0 + rows), n, rows, whi, wlo, xs, ws,
                            n == 0 and t == 0)

            for n in range(3):
                for t in range(NT):
                    product(n, t)
            for t in range(NT + 2):
                if t < NT:
                    product(3, t)
                if t >= 2:
                    pe.wait_ge(scaled, t - 1)
                    for h in range(2):
                        transpose_half(nc, m, pe, ring, index[("tr", t - 2, h)], xs_[t % 2], tile_cols(t - 2)[1], h)

        @block.vector
        def _(dve):
            out_split_engines(m, None, dve, None, src, names, whi, wlo, xs, ws, free)

            def add(n, t):
                rows = tile_cols(t)[1]
                i = index[("mm", n, t)]
                ring.wait_filled(dve, i)
                x = h1[0:rows, t, SEC * n:SEC * n + SEC]
                dve.tensor_tensor(x, x, ring.bank(i)[0:rows, 0:SEC], ALU.add).then_inc(ring.emptied["dve"], 1)

            for n in range(3):
                for t in range(NT):
                    if n == 0 and t in (0, 1, 5):
                        dve.wait_ge(row_loaded[(t + 3) // 4], 16)
                    add(n, t)
            for t in range(NT + 2):
                if t < NT:
                    add(3, t)
                    rstd_steps(dve, m, t, tile_cols(t)[1], sq_done, ms_done, rt_done, rs_done)
                if t >= 2:
                    empty_transposes(dve, m, ring, index[("tr", t - 2, 0)], t - 2, "od")

        @block.scalar
        def _(act):
            out_split_engines(m, act, None, None, src, names, whi, wlo, xs, ws, free)
            for t in range(NT):
                n = tile_cols(t)[1]
                act.wait_ge(ring.emptied["dve"], dcount(index[("mm", 3, t)]))
                act.activation(junk[0:n, :], h1[0:n, t, :], ACT.Square, accum_out=m.ss[0:n, t:t + 1]).then_inc(sq_done, 1)
                act.wait_ge(ms_done, t + 1)
                act.activation(m.rstd[0:n, t:t + 1], m.msq[0:n, t:t + 1], ACT.Sqrt).then_inc(rt_done, 1)
                act.wait_ge(rs_done, t + 1)
                if t >= 2:
                    act.wait_ge(ring.filled, index[("tr", t - 2, 1)] + 1)
                act.activation(xs_[t % 2][0:n, :], h1[0:n, t, :], ACT.Copy, scale=m.rstd[0:n, t:t + 1]).then_inc(scaled, 1)

        @block.gpsimd
        def _(pool):
            out_split_engines(m, None, None, pool, src, names, whi, wlo, xs, ws, free)


BAND = 3 * HD
NKEY = BAND + META


def odd_in_stage(nc, m, a, area):
    f = m.qkv1
    m.q1T = f[:, 0:8 * SEQ].rearrange("p (k l) -> p k l", k=8)
    m.k1T = f[:, 8192:8192 + 2 * L].rearrange("p (k l) -> p k l", k=2)
    m.v1T = f[:, 8192 + 2 * L:8192 + 3 * L]
    both = f[:, 8192 + 3 * L:8192 + 4 * L]
    frames = [(META, META + 512), (META + 512, L)]
    tiles = [dict(kind="n", section="okv", half=0, chunks=CHUNKS, gain=m.head_gain["odk"], dup=m.k1T,
                  dst=lambda c0, c1: both[:, c0:c1]),
             dict(kind="c", section="okv", half=1, chunks=CHUNKS, dst=lambda c0, c1: m.v1T[:, c0:c1])]
    for p in range(8):
        tiles.append(dict(kind="n", section=f"oq{p // 2}", half=p % 2, chunks=frames, gain=m.head_gain["odq"],
                          dst=lambda c0, c1, p=p: m.q1T[:, p, c0 - META:c1 - META]))
    for p in range(8):
        tiles.append(dict(kind="g", section=f"og{p // 2}", half=p % 2, chunks=frames,
                          dst=lambda c0, c1, p=p: m.mixT[:, p, c0:c1]))
    feature_stage(nc, m, area, tiles, m.xnT, m.section_at["oo1"])


def window_stage(nc, m, a, area):
    NQ = NT - 1
    NH, HG = 16, 4
    m.h1b = area.take("h1_frames_sb", NQ * D).rearrange("p (t n) -> p t n", t=NQ)
    m.h1_loaded = m.sem("h1_loaded")
    bias = area.take("bias", NH * NKEY).rearrange("p (h n) -> p h n", h=NH)
    kb = area.take("key_band", 2 * NQ * NKEY).rearrange("p (v i n) -> p v i n", v=2, i=NQ)
    vb = area.take("value_band", NQ * NKEY).rearrange("p (i n) -> p i n", i=NQ)
    dist = area.take("dist", NKEY)
    idist = area.take("idist", BAND).bitcast(I32)
    pbuf = [area.take(f"probs{i}", HG * NKEY).rearrange("p (h n) -> p h n", h=HG) for i in range(3)]
    vab = area.take("value_rows", NQ * 2 * P).rearrange("p (i b n) -> p i b n", i=NQ, b=2)
    ptb = [area.take(f"probs_t{i}", 1024).rearrange("p (b n) -> p b n", b=2) for i in range(2)]
    NB = NKEY - P
    slots = [dict(nm=m.small(HG), den=m.small(HG), es=m.small(HG), mx=m.small(HG)) for _ in range(3)]

    def place(j):
        return 2 * (j % 2) + j // 2

    its = [(i, hg) for i in range(NQ) for hg in range(NH // HG)]
    NI = len(its)
    zero, ready = m.sem("zero"), m.sem("ready")
    iota_done, steps, band_ready, vb_ready, vt_filled, vt_emptied = (
        m.sem(x) for x in ("iota_done", "steps", "band_ready", "vb_ready", "vt_filled", "vt_emptied"))
    scored, biased, maxed, exped, sink_exped, inverted, normed, turned, emptied_a, emptied_b, weighed, gated = (
        m.sem(x) for x in ("scored", "biased", "maxed", "exped", "sink_exped", "inverted", "normed", "turned",
                           "emptied_a", "emptied_b", "weighed", "gated"))
    sc = [m.wide[0], m.wide[1]]
    pta, ptb_ps = m.wide[2][:, 0:BANK], m.wide[2][:, BANK:2 * BANK]
    acc = [b[:, :] for b in m.bank]

    with nc.Block() as block:
        @block.sync
        def _(sp):
            for t in range(NQ):
                sp.dma_start(m.h1b[:, t, :], m.h1_dram[P * t:P * t + P, :]).then_inc(m.h1_loaded, 16)

        @block.gpsimd
        def _(pool):
            pool.iota(idist, pattern=[[-1, BAND]], base=HD, channel_multiplier=1).then_inc(iota_done, 1)
            for n, (i, hg) in enumerate(its):
                s = slots[n % 3]
                pool.wait_ge(inverted, n + 1)
                p = pbuf[n % 3]
                pool.tensor_tensor(p, p, bc(s["den"], 2, NKEY), ALU.mult).then_inc(normed, 1)

        @block.vector
        def _(dve):
            c = Chain(dve, steps)
            dve.memset(kb[:, :, 0, 0:HD], 0.0)
            dve.memset(vb[:, 0, 0:HD], 0.0)
            for i in range(NQ):
                lo = HD if i == 0 else 0
                c0 = META + P * i - HD + lo
                dve.tensor_copy(kb[:, :, i, lo:BAND], m.k1T[:, :, c0:c0 + BAND - lo])
                dve.tensor_copy(vb[:, i, lo:BAND], m.v1T[:, c0:c0 + BAND - lo])
            for kv in range(2):
                dve.tensor_copy(kb[:, kv, :, BAND:NKEY], bc(m.k1T[:, kv, 0:META], 1, NQ))
            c.link(dve.tensor_copy(vb[:, :, BAND:NKEY], bc(m.v1T[:, 0:META], 1, NQ)))
            dve.nop().then_inc(vb_ready, 1)
            dve.wait_ge(iota_done, 1)
            c.link(dve.memset(dist, 0.0))
            c.link(dve.tensor_copy(dist[:, 0:BAND], idist))
            c.link(dve.scalar_tensor_tensor(dist[:, 0:BAND], dist[:, 0:BAND], -1.0, dist[:, 0:BAND], ALU.mult, ALU.min))
            dve.memset(dist[0:HD, 2 * HD:BAND], -BIG)
            c.link(dve.memset(dist[HD:P, 0:HD], -BIG))
            for h in range(NH):
                ins = dve.tensor_scalar(bias[:, h // HG * HG + place(h % HG), :], dist, 2.0 ** (-8.0 * (h + 1) / NH), None, ALU.mult)
            c.link(ins)

            for n in range(NI + 3):
                if n < NI:
                    i, hg = its[n]
                    s = slots[n % 3]
                    p = pbuf[n % 3]
                    dve.wait_ge(scored, n + 1)
                    if n >= 3:
                        dve.wait_ge(turned, n - 2)
                    z = sc[n % 2][:, :].rearrange("p (b n) -> p b n", b=2)[:, :, 0:2 * NKEY]
                    dve.tensor_tensor(p.rearrange("p (b h) n -> p b (h n)", b=2), z,
                                      bias[:, HG * hg:HG * hg + HG, :].rearrange("p (b h) n -> p b (h n)", b=2),
                                      ALU.add).then_inc(biased, 1)
                    dve.wait_ge(biased, n + 1)
                    if i == 0:
                        c.link(dve.memset(p[:, :, 0:HD], -BIG))
                    c.link(dve.tensor_reduce(s["mx"], p, AX_X, ALU.max))
                    c.link(dve.scalar_tensor_tensor(s["nm"], s["mx"], -1.0, m.nsinks[:, HG * hg:HG * hg + HG],
                                                    ALU.mult, ALU.min))
                    dve.tensor_tensor(s["es"], m.sinks[:, HG * hg:HG * hg + HG], s["nm"], ALU.add).then_inc(maxed, 1)
                if 0 <= n - 1 < NI:
                    i, hg = its[n - 1]
                    s = slots[(n - 1) % 3]
                    dve.wait_ge(exped, HG * n)
                    dve.wait_ge(sink_exped, n)
                    c.link(dve.tensor_tensor(s["den"], s["den"], s["es"], ALU.add))
                    dve.reciprocal(s["den"], s["den"]).then_inc(inverted, 1)
                if 0 <= n - 2 < NI:
                    k = n - 2
                    dve.wait_ge(turned, k + 1)
                    if k >= 2:
                        dve.wait_ge(weighed, k - 1)
                    dve.tensor_copy(ptb[k % 2][0:NB, 1, :], ptb_ps[0:NB, :]).then_inc(emptied_b, 1)
                if 0 <= n - 3 < NI:
                    k = n - 3
                    i, hg = its[k]
                    dve.wait_ge(weighed, k + 1)
                    g = m.mixT[:, 2 * hg:2 * hg + 2, META + P * i:META + P * i + P]
                    dve.tensor_tensor(g, g, acc[k % 2][:, 0:2 * P].rearrange("p (a q) -> p a q", a=2), ALU.mult
                                      ).then_inc(gated, 1)

        @block.scalar
        def _(act):
            for i in range(NQ):
                act.wait_ge(vt_filled, i + 1)
                b = m.banks[i % 4]
                act.activation(vab[:, i, 0, :], b[:, 0:P], ACT.Copy).then_inc(vt_emptied, 1)
                act.activation(vab[0:NB, i, 1, :], b[0:NB, P:2 * P], ACT.Copy).then_inc(vt_emptied, 1)
            for n in range(NI + 2):
                if n < NI:
                    s = slots[n % 3]
                    p = pbuf[n % 3]
                    act.wait_ge(maxed, n + 1)
                    if n >= 3:
                        act.wait_ge(normed, n - 2)
                    for j in range(HG):
                        act.activation(p[:, j, :], p[:, j, :], ACT.Exp, bias=s["nm"][:, j:j + 1],
                                       accum_out=s["den"][:, j:j + 1]).then_inc(exped, 1)
                    act.activation(s["es"], s["es"], ACT.Exp).then_inc(sink_exped, 1)
                if n >= 2:
                    k = n - 2
                    act.wait_ge(turned, k + 1)
                    if k >= 2:
                        act.wait_ge(weighed, k - 1)
                    act.activation(ptb[k % 2][:, 0, :], pta, ACT.Copy).then_inc(emptied_a, 1)

        @block.tensor
        def _(pe):
            pe.wait_ge(vb_ready, 1)
            for i in range(NQ):
                if i >= 4:
                    pe.wait_ge(vt_emptied, 2 * (i - 3))
                b = m.banks[i % 4]
                nc.tensor.transpose(b[:, 0:P], vb[:, i, 0:P], m.ident[:, :])
                nc.tensor.transpose(b[0:NB, P:2 * P], vb[:, i, P:NKEY], m.ident[:, :]).then_inc(vt_filled, 1)
            pe.wait_ge(vt_emptied, 2 * NQ)

            def score(n):
                i, hg = its[n]
                if n >= 2:
                    pe.wait_ge(biased, n - 1)
                for j in range(HG):
                    h = HG * hg + j
                    r = slice(HD * (h % 2), HD * (h % 2) + HD)
                    o = BANK * (j % 2) + NKEY * (j // 2)
                    dst = sc[n % 2][:, o:o + NKEY]
                    last = nc.tensor.matmul(dst, m.q1T[r, h // 2, P * i:P * i + P], kb[r, h // 8, i, :], start=True, stop=True)
                last.then_inc(scored, 1)

            def turn(n):
                pe.wait_ge(normed, n + 1)
                if n >= 1:
                    pe.wait_ge(emptied_a, n)
                    pe.wait_ge(emptied_b, n)
                p = pbuf[n % 3]
                for j in range(HG):
                    nc.tensor.transpose(pta[:, P * j:P * j + P], p[:, place(j), 0:P], m.ident[:, :])
                    last = nc.tensor.transpose(ptb_ps[0:NB, P * j:P * j + P], p[:, place(j), P:NKEY], m.ident[:, :])
                last.then_inc(turned, 1)

            def weigh(n):
                i, hg = its[n]
                pe.wait_ge(emptied_a, n + 1)
                pe.wait_ge(emptied_b, n + 1)
                if n >= 2:
                    pe.wait_ge(gated, n - 1)
                for j in range(HG):
                    h = HG * hg + j
                    kv = h // 8
                    dst = acc[n % 2][HD * (j % 2):HD * (j % 2) + HD, P * (j // 2):P * (j // 2) + P]
                    nc.tensor.matmul(dst, vab[:, i, 0, HD * kv:HD * kv + HD], ptb[n % 2][:, 0, P * j:P * j + P],
                                     start=True, stop=False)
                    last = nc.tensor.matmul(dst, vab[0:NB, i, 1, HD * kv:HD * kv + HD], ptb[n % 2][0:NB, 1, P * j:P * j + P],
                                            start=False, stop=True)
                last.then_inc(weighed, 1)

            for n in range(NI + 3):
                if n < NI:
                    score(n)
                if 0 <= n - 2 < NI:
                    turn(n - 2)
                if 0 <= n - 3 < NI:
                    weigh(n - 3)


def odd_out_stage(nc, m, a, out, area):
    NQ = NT - 1
    src = split_mix(m, area, 1)
    area.take("gap", HEAD - 8 * L)
    area.take("h1_loaded", NQ * D)
    whi, wlo = out_weights(area, 1)
    names = [f"oo{n}" for n in range(4)]
    ring = m.ring(m.banks, ["dve"] * (4 * NQ))
    stored = m.sem("stored")
    xs = [m.sem(x) for x in ("mix_hi_act", "mix_hi_dve", "mix_lo_pool", "mix_lo_dve")]
    ws = [m.sem(x) for x in ("w_hi", "w_lo", "w_first_hi", "w_first")]
    for n in range(4):
        m.section_end[names[n]] = (ws[1], n) if n else (ws[3], 1)
    free = lambda n: (ring.filled, NQ * (n + 1))

    with nc.Block() as block:
        @block.tensor
        def _(pe):
            for n in range(4):
                wait_out_weights(pe, ws, n)
                for t in range(NQ):
                    c0 = META + P * t
                    out_product(nc, m, pe, ring, NQ * n + t, slice(c0, c0 + P), n, P, whi, wlo, xs, ws, n == 0 and t == 0)

        @block.vector
        def _(dve):
            out_split_engines(m, None, dve, None, src, names, whi, wlo, xs, ws, free, META)
            dve.wait_ge(m.h1_loaded, 16 * NQ)
            for n in range(4):
                for t in range(NQ):
                    i = NQ * n + t
                    ring.wait_filled(dve, i)
                    x = m.h1b[:, t, SEC * n:SEC * n + SEC]
                    dve.tensor_tensor(x, x, ring.bank(i)[:, 0:SEC], ALU.add).then_inc(ring.emptied["dve"], 1)

        @block.scalar
        def _(act):
            out_split_engines(m, act, None, None, src, names, whi, wlo, xs, ws, free, META)

        @block.gpsimd
        def _(pool):
            out_split_engines(m, None, None, pool, src, names, whi, wlo, xs, ws, free, META)

        @block.sync
        def _(sp):
            send_sections(m, sp, len(m.sections) - 1)
            for t in range(NQ):
                sp.wait_ge(ring.emptied["dve"], 3 * NQ + t + 1)
                sp.dma_start(out[0, P * t:P * t + P, :], m.h1b[:, t, :]).then_inc(stored, 16)
            sp.wait_ge(stored, 16 * NQ)




_INS = ["x", "meta_tokens", "ev_norm", "ev_w_in", "ev_q_norm", "ev_k_norm", "ev_log_dt", "ev_a_re", "ev_a_im",
        "ev_b_re", "ev_b_im", "ev_c_re", "ev_c_im", "ev_d", "ev_w_glu", "ev_b_glu", "ev_w_out", "od_norm",
        "od_w_in", "od_q_norm", "od_k_norm", "od_sinks", "od_w_out"]


def kernel(**inputs):
    import numpy as _np
    import concourse.bacc as _bacc
    from concourse import mybir as _mybir
    from concourse.bass_utils import run_bass_kernel_spmd as _run

    nc = _bacc.Bacc("TRN2", target_bir_lowering=False, num_devices=1)
    arrays, aps = {}, {}
    for name in _INS:
        v = _np.ascontiguousarray(inputs[name])
        arrays[f"in_{name}_dram"] = v
        aps[name] = nc.dram_tensor(f"in_{name}_dram", v.shape, _mybir.dt.from_np(v.dtype), kind="ExternalInput").ap()
    out = nc.dram_tensor("out_0_dram", (1, 1024, 1024), _mybir.dt.float32, kind="ExternalOutput").ap()
    kernel_program(nc, aps, out)
    r = _run(nc, [arrays], core_ids=[0])
    return r.results[0]["out_0_dram"]
```

```python
from contextlib import ExitStack

import concourse.bass as bass
from concourse import mybir

ALU = mybir.AluOpType
ACT = mybir.ActivationFunctionType
F32 = mybir.dt.float32
F32R = mybir.dt.float32r
BF16 = mybir.dt.bfloat16
I32 = mybir.dt.int32
AX_X = mybir.AxisListType.X

P = 128
D = 1024
KD = D // P
META = 16
SEQ = 1024
L = META + SEQ
NT = 1 + SEQ // P
HD = 64
EPS = 1e-6
BANK = 512

NPAIR = 4
G, GC, NST = 32, 16, 64
G2 = G // 2
TC = 8
NCH = L // TC
MCH = META // TC
LOG_SCALE = 10
TAYLOR = 7
CHUNKS = [(0, 400), (400, 784), (784, 1040)]

QUERIES = [(656, 1040), (144, 656), (0, 144)]
NZ, NLOG, NSOFT, NSPLIT, NTOTAL, NWEIGHT, LAG = 6, 4, 6, 7, 6, 4, 4
DVE_CAPS_EVERY = 3
SEC = 256
BIG = 1e30
MASK = 2.0 ** 99


def tile_cols(t):
    return (0, META) if t == 0 else (META + P * (t - 1), P)


def bc(ap, axis, n):
    v = ap.unsqueeze(axis)
    shape = list(v.shape)
    shape[axis] = n
    return v.broadcast_to(tuple(shape))


class Ring:

    def __init__(self, sems, banks, emptied_by):
        self.filled, self.emptied = sems["filled"], sems
        self.banks, self.by = banks, emptied_by

    def bank(self, n):
        return self.banks[n % len(self.banks)]

    def wait_free(self, pe, n):
        m = n - len(self.banks)
        if m >= 0:
            e = self.by[m]
            pe.wait_ge(self.emptied[e], self.by[:m + 1].count(e))

    def wait_filled(self, eng, n):
        eng.wait_ge(self.filled, n + 1)


class Chain:

    def __init__(self, eng, sem):
        self.eng, self.sem, self.n = eng, sem, 0

    def link(self, ins):
        self.n += 1
        ins.then_inc(self.sem, 1)
        self.eng.wait_ge(self.sem, self.n)


class K:
    pass


def plan_memory(nc, ctx):
    m = K()

    def sb(name, cols, dt=F32, parts=P):
        return ctx.enter_context(nc.sbuf_tensor(name, [parts, cols], dt))

    m.ident = sb("ident", P)
    m.tri = sb("tri", P)
    m.ones = sb("ones", P)
    m.headmean = sb("headmean", P)
    m.kvcopy = sb("kvcopy", 2 * P)
    m.identb = sb("identb", P, BF16)
    m.negmask = sb("negmask", P, BF16)
    m.sm = sb("sm", 960)
    m.wst = sb("wst", 2 * KD * SEC)
    m.bank = [ctx.enter_context(nc.psum_tensor(f"bank{i}", [P, BANK], F32)) for i in range(2)]
    m.wide = [ctx.enter_context(nc.psum_tensor(f"wide{i}", [P, 2 * BANK], F32)) for i in range(3)]
    m.banks = [m.wide[i][:, h * BANK:(h + 1) * BANK] for i in range(3) for h in range(2)] + \
              [b[:, :] for b in m.bank]
    m.small_at = 0

    def small(n):
        m.small_at += n
        assert m.small_at <= 960
        return m.sm[:, m.small_at - n:m.small_at]

    m.gain = {n: small(KD) for n in ("ev", "od")}
    m.head_gain = {n: small(1) for n in ("evq", "evk", "odq", "odk")}
    m.eps = small(1)
    m.bglu = small(4)
    m.sinks, m.nsinks, m.sinks_in = small(16), small(16), small(16)
    m.ss = small(16)
    m.rstd = small(16)
    m.msq = small(16)
    m.small = small
    return m


class Area:

    def __init__(self, nc):
        self.nc, self.ctx = nc, ExitStack()

    def take(self, name, cols, dt=F32):
        return self.ctx.enter_context(self.nc.sbuf_tensor(name, [P, cols], dt))[:, :]

    def close(self):
        self.ctx.close()


HEAD = 8 * L + NT * 512


def split_tiles(act, dve, pool, src, hi, lo, sems, first=0):
    hi_act, hi_dve, lo_pool, lo_dve = sems
    n_act = n_dve = 0
    for c0, c1 in CHUNKS:
        cols = slice(max(c0, first), c1)
        for k in range(KD):
            s, h, l = (x[:, k, cols] for x in (src, hi, lo))
            if k in ON_ACT:
                n_act += 1
                if act:
                    act.activation(h, s, ACT.Copy).then_inc(hi_act, 1)
                if pool:
                    pool.wait_ge(hi_act, n_act)
                    pool.tensor_tensor(l, s, h.bitcast(F32), ALU.subtract).then_inc(lo_pool, 1)
            else:
                n_dve += 1
                if dve:
                    dve.tensor_copy(h, s).then_inc(hi_dve, 1)
                    dve.wait_ge(hi_dve, n_dve)
                    dve.tensor_tensor(l, s, h.bitcast(F32), ALU.subtract).then_inc(lo_dve, 1)


ON_ACT = (0, 2, 4)


def wait_split(pe, k, sems, end):
    chunk = [end <= c1 for _, c1 in CHUNKS].index(True)
    n = len(ON_ACT) * chunk + sum(1 for j in ON_ACT if j <= k)
    pe.wait_ge(sems[2], n)
    if KD * chunk + k + 1 - n:
        pe.wait_ge(sems[3], KD * chunk + k + 1 - n)


def split_product(nc, out, lhs, rhs, nk=KD, before=None):
    for k in range(nk):
        if before:
            before(k)
        for n, (i, j) in enumerate(((0, 0), (0, 1), (1, 0))):
            ins = nc.tensor.matmul(out, lhs(k)[i], rhs(k)[j], start=(k == 0 and n == 0), stop=(k == nk - 1 and n == 2))
    return ins


def kernel_program(nc, a, out):
    ctx = ExitStack()
    with ctx:
        m = plan_memory(nc, ctx)
        made = [0]

        def sem(name):
            made[0] += 1
            return ctx.enter_context(nc.semaphore(f"{name}_{made[0]}"))

        def ring(banks, by):
            return Ring({k: sem(k) for k in ["filled"] + sorted(set(by))}, banks, by)

        m.sem, m.ring = sem, ring
        ctx.enter_context(nc.allow_non_contiguous_dma(reason="small per-feature parameters"))
        views(m, a)
        mixes = Area(nc)
        m.mix = mixes.take("mix", 8 * L)
        area = Area(nc)
        m.f1, m.xn, m.f2 = area.take("s5_a", HEAD), area.take("xn", KD * L), area.take("s5_b", 17056)
        m.xnT = m.xn.rearrange("p (k l) -> p k l", k=KD)
        m.mixT = m.mix.rearrange("p (k l) -> p k l", k=8)
        norm_stage(nc, m, a)
        s5_input_stage(nc, m, a)
        s5_stage(nc, m, a)
        area.close()
        qkv_area = Area(nc)
        m.qk, m.vrows = qkv_area.take("qk", 8 * L), qkv_area.take("vrows", NT * 512)
        area = Area(nc)
        split_area(m, area, 0)
        qkv_stage(nc, m, a, area)
        area.close()
        area = Area(nc)
        stick_breaking_stage(nc, m, a, area)
        area.close()
        qkv_area.close()
        mixes.close()

        mixes = Area(nc)
        m.mixlo = mixes.take("mix_lo0", 8 * L, F32R)
        area = Area(nc)
        even_out_stage(nc, m, a, area)
        area.close()
        mixes.close()
        mixes = Area(nc)
        m.mix = mixes.take("mix1", 8 * L)
        m.mixT = m.mix.rearrange("p (k l) -> p k l", k=8)
        head = Area(nc)
        m.qkv1 = head.take("qkv1", HEAD)
        area = Area(nc)
        split_area(m, area, 1)
        odd_in_stage(nc, m, a, area)
        area.close()
        area = Area(nc)
        window_stage(nc, m, a, area)
        area.close()
        head.close()
        mixes.close()
        mixes = Area(nc)
        m.mixlo = mixes.take("mix_lo1", 8 * L, F32R)
        area = Area(nc)
        odd_out_stage(nc, m, a, out, area)
        area.close()
        mixes.close()


def split_area(m, area, layer):
    m.xlo = area.take(f"xn_lo{layer}", KD * L, F32R).rearrange("p (k l) -> p k l", k=KD)
    m.xhi = area.take(f"xn_hi{layer}", KD * L, F32R).rearrange("p (k l) -> p k l", k=KD)
    m.whi = [area.take(f"w_hi{layer}{i}", KD * P, F32R).rearrange("p (k n) -> p k n", k=KD) for i in range(2)]
    m.wlo = [area.take(f"w_lo{layer}{i}", KD * P, F32R).rearrange("p (k n) -> p k n", k=KD) for i in range(2)]


def views(m, a):
    w0 = a["ev_w_in"][0].rearrange("(k p) n -> p k n", p=P)
    w1 = a["od_w_in"][0].rearrange("(k p) n -> p k n", p=P)
    sections = []

    def add(name, w, c0):
        sections.append((name, w[:, :, c0:c0 + SEC]))

    add("u0", w0, 2048), add("u1", w0, 2304)
    for s in range(2):
        add(f"gs{s}", w0, 2560 + SEC * s)
    sections.append(("glu", a["ev_w_glu"][0].rearrange("(k p) n -> p k n", p=P)))
    for i, name in enumerate(("q0", "q1", "k0", "k1", "v0", "v1")):
        add(name, w0, SEC * i)
    for s in range(2):
        add(f"gb{s}", w0, 1536 + SEC * s)
    wo = [a[n][0].rearrange("(k p) n -> p k n", p=P) for n in ("ev_w_out", "od_w_out")]
    for s in range(4):
        add(f"eo{s}", wo[0], SEC * s)
    add("okv", w1, 1024)
    for s in range(4):
        add(f"oq{s}", w1, SEC * s)
    for s in range(4):
        add(f"og{s}", w1, 1280 + SEC * s)
    for s in range(4):
        add(f"oo{s}", wo[1], SEC * s)
    m.sections = sections
    m.section_at = {n: i for i, (n, _) in enumerate(sections)}
    m.section_loaded = [m.sem("section_loaded") for _ in range(2)]
    m.section_end = {}
    m.sections_sent = 0


def section(m, name):
    i = m.section_at[name]
    k, n = m.sections[i][1].shape[1:]
    return m.wst[:, (i % 2) * KD * SEC:(i % 2 + 1) * KD * SEC].rearrange("p (k n) -> p k n", k=k)


def send_sections(m, sp, upto):
    while m.sections_sent <= min(upto, len(m.sections) - 1):
        i = m.sections_sent
        name, src = m.sections[i]
        if i >= 2:
            sp.wait_ge(*m.section_end[m.sections[i - 2][0]])
        sp.dma_start(section(m, name), src).then_inc(m.section_loaded[i % 2], 16)
        m.sections_sent += 1


def wait_section(m, pe, name):
    i = m.section_at[name]
    pe.wait_ge(m.section_loaded[i % 2], 16 * (i // 2 + 1))


def norm_stage(nc, m, a):
    f = m.f1
    rows = [f[:, 0:D]] + [m.mix[:, D * (t - 1):D * t] for t in range(1, NT)]
    row_loaded = [m.sem("row_loaded") for _ in range(NT)]
    consts, params = m.sem("consts"), m.sem("params")
    junk = [f[:, D * (2 + i):D * (3 + i)] for i in range(2)]
    nfill = 2 * NT
    ring = m.ring(m.banks, ["dve"] * nfill)
    sq_done, ms_done, rt_done, rs_done, scaled = (m.sem(x) for x in ("sq_done", "ms_done", "rt_done", "rs_done", "scaled"))
    zi, chain, gain_loaded = m.sem("zi"), m.sem("chain"), m.sem("gain_loaded")

    with nc.Block() as block:
        @block.sync
        def _(sp):
            sp.dma_start(rows[0][0:META, :], a["meta_tokens"]).then_inc(row_loaded[0], 16)
            for t in range(1, NT):
                sp.dma_start(rows[t], a["x"][0, P * (t - 1):P * t, :]).then_inc(row_loaded[t], 16)
            for n, src in (("evq", "ev_q_norm"), ("evk", "ev_k_norm"), ("odq", "od_q_norm"), ("odk", "od_k_norm")):
                for h in range(2):
                    sp.dma_start(m.head_gain[n][HD * h:HD * h + HD, :],
                                 a[src][0].rearrange("(p o) -> p o", o=1)).then_inc(params, 16)
            sp.dma_start(m.gain["od"], a["od_norm"][0].rearrange("(k p) -> p k", p=P)).then_inc(params, 16)
            sp.dma_start(m.bglu, a["ev_b_glu"][0].rearrange("(k p) -> p k", p=P)).then_inc(params, 16)
            sp.dma_start(m.sinks_in, a["od_sinks"][0:1, :].broadcast_to((P, 16))).then_inc(params, 16)
            send_sections(m, sp, 1)

        @block.gpsimd
        def _(pool):
            pool.memset(m.ident[:, :], 0.0).then_inc(zi, 1)
            pool.memset(m.identb[:, :], 0.0).then_inc(zi, 1)
            pool.memset(m.tri[:, :], -1.0).then_inc(zi, 1)
            pool.memset(m.negmask[:, :], -BIG).then_inc(zi, 1)
            pool.memset(m.ones[:, :], -1.0).then_inc(consts, 1)
            pool.wait_ge(zi, 4)
            for t in (m.ident, m.identb):
                pool.affine_select(out=t[:, :], in_=t[:, :], compare_op=ALU.not_equal, fill=1.0,
                                   base=0, pattern=[[-1, P]], channel_multiplier=1).then_inc(consts, 1)
            for t in (m.tri, m.negmask):
                pool.affine_select(out=t[:, :], in_=t[:, :], compare_op=ALU.is_ge, fill=0.0,
                                   base=0, pattern=[[-1, P]], channel_multiplier=1).then_inc(consts, 1)
            pool.wait_ge(consts, 5)

        @block.scalar
        def _(act):
            act.dma_start(m.gain["ev"], a["ev_norm"][0].rearrange("(k p) -> p k", p=P)).then_inc(gain_loaded, 16)
            act.wait_ge(chain, 1)
            for t in range(NT + 1):
                if t < NT:
                    n = tile_cols(t)[1]
                    act.wait_ge(row_loaded[t], 16)
                    act.activation(junk[t % 2][0:n, :], rows[t][0:n, :], ACT.Square,
                                   accum_out=m.ss[0:n, t:t + 1]).then_inc(sq_done, 1)
                if t >= 1:
                    n = tile_cols(t - 1)[1]
                    act.wait_ge(ms_done, t)
                    act.activation(m.rstd[0:n, t - 1:t], m.msq[0:n, t - 1:t], ACT.Sqrt).then_inc(rt_done, 1)

        @block.tensor
        def _(pe):
            pe.wait_ge(consts, 5)
            for t in range(NT):
                n = tile_cols(t)[1]
                pe.wait_ge(scaled, t + 1)
                for half in range(2):
                    transpose_half(nc, m, pe, ring, 2 * t + half, rows[t], n, half)

        @block.vector
        def _(dve):
            c = Chain(dve, chain)
            c.link(dve.memset(m.ss, 1.0))
            dve.memset(m.eps, EPS)
            dve.memset(m.headmean[:, :], 0.0)
            c.link(dve.memset(m.kvcopy[:, :], 0.0))
            for h in range(2):
                dve.memset(m.headmean[HD * h:HD * h + HD, HD * h:HD * h + HD], 1.0 / HD)
            dve.wait_ge(consts, 5)
            for v in range(2):
                for h in range(2):
                    dve.tensor_copy(m.kvcopy[:, P * v + HD * h:P * v + HD * h + HD], m.ident[:, HD * v:HD * v + HD])
            dve.wait_ge(gain_loaded, 16)
            for t in range(NT + 1):
                if t < NT:
                    n = tile_cols(t)[1]
                    dve.wait_ge(sq_done, t + 1)
                    dve.tensor_scalar(m.msq[0:n, t:t + 1], m.ss[0:n, t:t + 1], 1.0 / D, EPS,
                                      ALU.mult, ALU.add).then_inc(ms_done, 1)
                if t >= 1:
                    n = tile_cols(t - 1)[1]
                    dve.wait_ge(rt_done, t)
                    dve.reciprocal(m.rstd[0:n, t - 1:t], m.rstd[0:n, t - 1:t]).then_inc(rs_done, 1)
                    dve.wait_ge(rs_done, t)
                    dve.tensor_scalar(rows[t - 1][0:n, :], rows[t - 1][0:n, :], m.rstd[0:n, t - 1:t], None,
                                      ALU.mult).then_inc(scaled, 1)
                if t >= 2:
                    empty_transposes(dve, m, ring, 2 * (t - 2), t - 2, "ev")
            empty_transposes(dve, m, ring, 2 * (NT - 1), NT - 1, "ev")
            dve.wait_ge(params, 16 * 11)
            for n in ("evq", "odq"):
                c.link(dve.tensor_scalar(m.head_gain[n], m.head_gain[n], HD ** -0.5, None, ALU.mult))
            perm = m.sinks_in.rearrange("p (g h b) -> p g b h", g=4, b=2)
            dve.tensor_copy(m.sinks.rearrange("p (g b h) -> p g b h", g=4, b=2), perm)
            c.link(dve.tensor_scalar(m.nsinks.rearrange("p (g b h) -> p g b h", g=4, b=2), perm, -1.0, None, ALU.mult))


def rstd_steps(dve, m, t, n, sq_done, ms_done, rt_done, rs_done):
    dve.wait_ge(sq_done, t + 1)
    dve.tensor_scalar(m.msq[0:n, t:t + 1], m.ss[0:n, t:t + 1], 1.0 / D, EPS, ALU.mult, ALU.add).then_inc(ms_done, 1)
    dve.wait_ge(rt_done, t + 1)
    dve.reciprocal(m.rstd[0:n, t:t + 1], m.rstd[0:n, t:t + 1]).then_inc(rs_done, 1)


def transpose_half(nc, m, pe, ring, fill, row, n, half):
    ring.wait_free(pe, fill)
    for j in range(4):
        k = 4 * half + j
        last = nc.tensor.transpose(ring.bank(fill)[:, j * n:(j + 1) * n], row[0:n, P * k:P * k + P], m.ident[0:n, 0:n])
    last.then_inc(ring.filled, 1)


def empty_transposes(dve, m, ring, fill, t, gain):
    c0, n = tile_cols(t)
    for half in range(2):
        ring.wait_filled(dve, fill + half)
        dve.tensor_tensor(m.xnT[:, 4 * half:4 * half + 4, c0:c0 + n],
                          ring.bank(fill + half)[:, 0:4 * n].rearrange("p (k n) -> p k n", k=4),
                          bc(m.gain[gain][:, 4 * half:4 * half + 4], 2, n), ALU.mult).then_inc(ring.emptied["dve"], 1)


def row_product(nc, m, pe, out, cols, w, c0, c1):
    for k in range(KD):
        ins = nc.tensor.matmul(out, m.xnT[:, k, cols], w[:, k, c0:c1], start=(k == 0), stop=(k == KD - 1))
    return ins


def col_product(nc, m, pe, out, lhs, rhs, nk=KD):
    for k in range(nk):
        ins = nc.tensor.matmul(out, lhs(k), rhs(k), start=(k == 0), stop=(k == nk - 1))
    return ins


def s5_views(m):
    at = [0, 0]

    def take(n, where=1):
        at[where] += n
        return (m.f1, m.f2)[where][:, at[where] - n:at[where]]

    m.urow = take(TC * SEC, 0).rearrange("p (g j c) -> p g j c", g=G2, j=TC)
    m.uj = take(G * NCH, 0).rearrange("p (g c) -> p g c", g=G)
    m.w1 = take(G2 * 2 * P, 0).rearrange("p (g r s) -> p g r s", g=G2, r=2)
    m.ca = take(2 * G2 * 9 * GC).rearrange("p (r g k c) -> p r g k c", r=2, g=G2, k=9)
    m.w3 = take(G * P).rearrange("p (g n) -> p g n", g=G)
    v = take(2 * G2 * (NCH + 1))
    m.v = v.rearrange("p (r g c) -> p r g c", r=2, g=G2)
    m.ba = v[:, 0:2 * G2 * TC * GC].rearrange("p (r g j c) -> p r g j c", r=2, g=G2, j=TC)
    ptab = take(2 * G2 * NCH)
    m.turn = ptab.rearrange("p (r g c) -> p r g c", r=2, g=G2)
    m.yT = ptab.rearrange("p (k l) -> p k l", k=4)
    m.tmp = take(2016, 0)
    m.radius = m.small(G2)


def s5_input_stage(nc, m, a):
    s5_views(m)
    mx = m.mix
    t4 = [mx[:, 1024 * i:1024 * i + 1024] for i in range(4)]
    zt = m.zt = mx[0:GC, 0:4096].rearrange("p (g n) -> p g n", g=G)
    pt = [mx[:, 4096 + 576 * i:4096 + 576 * (i + 1)] for i in range(4)]
    braw = mx[:, 6400:6912].rearrange("p (r g c) -> p r g c", r=2, g=G2)
    craw = mx[:, 6912:7424].rearrange("p (r t s) -> p r t s", r=2, t=2)
    arow = mx[0:G2, 7424:7424 + 384].rearrange("p (i s) -> p i s", i=3)
    ldt = mx[0:G2, 7808:7810]
    um16 = mx[0:META, 7810:7810 + SEC]
    um2 = m.w3.rearrange("p g n -> p (g n)")[0:MCH, 0:TC * SEC].rearrange("p (g j c) -> p g j c", g=G2, j=TC)
    dcol = mx[0:GC, 8066:8066 + G]
    sm = mx[:, 8100:8320]

    small = [m.small(G2) for _ in range(12)]
    ar, ai, dt, zr, zi, er, ei, s1, s2, s3, s4, s5 = small
    pw = m.small(9 * 2 * G2).rearrange("p (k r g) -> p k r g", k=9, r=2)

    param_loaded, c_loaded, b_loaded, d_loaded = (m.sem(x) for x in ("param_loaded", "c_loaded", "b_loaded", "d_loaded"))
    um_evac, um_moved = m.sem("um_evac"), m.sem("um_moved")
    arow_ready, dt_ready, steps = m.sem("arow_ready"), m.sem("dt_ready"), m.sem("steps")
    power_ready, ba_ready, ca_ready, zt_free, m.z_diag, m.w3_zero, m.w3_moved = (
        m.sem(x) for x in ("power_ready", "ba_ready", "ca_ready", "zt_free", "z_diag", "w3_zero", "w3_moved"))
    root_ready, sq_ready = m.sem("root_ready"), m.sem("sq_ready")
    ca_steps, c_copied = m.sem("ca_steps"), m.sem("c_copied")

    FA, FC = 1, 11
    fm = lambda h: (0, 12)[h]
    fu = lambda h, jp: (2, 13)[h] + jp
    ft = lambda h, q: (6, 17)[h] + q
    ftm = lambda h: (10, 21)[h]
    FW1 = 22
    FZ = FW1 + 8
    ring = m.ring(m.banks, ["act"] * (FZ + 8))
    for h in range(2):
        m.section_end[f"u{h}"] = (ring.filled, fu(h, TC // 2 - 1) + 1)

    with nc.Block() as block:
        @block.sync
        def _(sp):
            sp.dma_start(arow[:, 0, :], a["ev_a_re"][0].rearrange("(g e) n -> g (e n)", e=2)).then_inc(param_loaded, 16)
            sp.dma_start(arow[:, 1, :], a["ev_a_im"][0].rearrange("(g e) n -> g (e n)", e=2)).then_inc(param_loaded, 16)
            sp.dma_start(ldt, a["ev_log_dt"][0].rearrange("(g e) -> g e", e=2)).then_inc(param_loaded, 16)
            for r, name in enumerate(("ev_b_re", "ev_b_im")):
                for e in range(2):
                    sp.dma_start(braw[NST * e:NST * e + NST, r],
                                 a[name][0].rearrange("(g e) n c -> e n g c", e=2)[e]).then_inc(b_loaded, 16)
            for r, name in enumerate(("ev_c_re", "ev_c_im")):
                c = a[name][0].rearrange("(t g e) c n -> t g c e n", t=2, e=2)
                for t in range(2):
                    for g in range(G2 // 2):
                        sp.dma_start(craw[GC * g:GC * g + GC, r, t].rearrange("p (e n) -> p e n", e=2),
                                     c[t, g]).then_inc(c_loaded, 16)
            sp.dma_start(dcol, a["ev_d"][0].rearrange("g c -> c g")).then_inc(d_loaded, 16)
            for h in range(2):
                sp.wait_ge(um_evac, h + 1)
                for c in range(MCH):
                    for j in range(TC):
                        sp.dma_start(um2[c:c + 1, :, j], um16[TC * c + j:TC * c + j + 1, :]
                                     .rearrange("p (g c) -> p g c", c=GC)).then_inc(um_moved, 16)
            send_sections(m, sp, 3)

        @block.tensor
        def _(pe):
            def t_group(fill, dsts):
                ring.wait_free(pe, fill)
                for dst, src, ident in dsts:
                    last = nc.tensor.transpose(dst, src, ident)
                last.then_inc(ring.filled, 1)

            for h in range(2):
                w = section(m, f"u{h}")
                wait_section(m, pe, f"u{h}")
                ring.wait_free(pe, fm(h))
                row_product(nc, m, pe, ring.bank(fm(h))[0:META, 0:SEC], slice(0, META), w, 0, SEC).then_inc(ring.filled, 1)
                if h == 0:
                    pe.wait_ge(arow_ready, 1)
                    t_group(FA, [(ring.bank(FA)[:, G2 * i:G2 * i + G2], arow[:, i, :], m.ident[0:G2, 0:G2])
                                 for i in range(3)])
                for jp in range(TC // 2):
                    ring.wait_free(pe, fu(h, jp))
                    for e in range(2):
                        j = 2 * jp + e
                        last = row_product(nc, m, pe, ring.bank(fu(h, jp))[:, e * SEC:e * SEC + SEC],
                                           slice(META + j, L, TC), w, 0, SEC)
                    last.then_inc(ring.filled, 1)
                pe.wait_ge(ring.emptied["act"], fu(h, 3) + 1)
                for q in range(4):
                    t_group(ft(h, q), [(ring.bank(ft(h, q))[:, P * i:P * i + P],
                                        m.urow[:, 4 * q + i], m.ident[:, :])
                                       for i in range(4)])
                pe.wait_ge(um_moved, 16 * META * (h + 1))
                t_group(ftm(h), [(ring.bank(ftm(h))[:, MCH * g:MCH * g + MCH], um2[:, g],
                                  m.ident[0:MCH, 0:MCH]) for g in range(16)])
                if h == 0:
                    pe.wait_ge(c_loaded, 16 * 2 * G2)
                    t_group(FC, [(ring.bank(FC)[:, P * (2 * r + t):P * (2 * r + t) + P], craw[:, r, t], m.ident[:, :])
                                 for r in range(2) for t in range(2)])
            pe.wait_ge(ba_ready, 1)
            for q in range(8):
                t_group(FW1 + q, [(ring.bank(FW1 + q)[:, P * (2 * i + r):P * (2 * i + r) + P],
                                   m.ba[:, r, 2 * q + i], m.ident[:, :]) for i in range(2) for r in range(2)])
            pe.wait_ge(ca_ready, 1)
            for q in range(8):
                ring.wait_free(pe, FZ + q)
                for i in range(4):
                    g = 8 * (q // 2) + 2 * i + q % 2
                    rows = slice(NST * (g % 2), NST * (g % 2) + NST)
                    for r in range(2):
                        last = nc.tensor.matmul(ring.bank(FZ + q)[0:GC, P * i:P * i + P], m.ba[rows, r, g // 2, TC - 1],
                                                m.ca[rows, r, g // 2, 0:TC], start=(r == 0), stop=(r == 1))
                last.then_inc(ring.filled, 1)

        @block.scalar
        def _(act):
            def copy(dst, src, s, n=1):
                return act.activation(dst, src, ACT.Copy).then_inc(s, n)
            for h in range(2):
                ring.wait_filled(act, fm(h))
                if h:
                    act.wait_ge(um_moved, 16 * META * h)
                act.activation(um16, ring.bank(fm(h))[0:META, 0:SEC], ACT.Copy).then_inc(um_evac, 1)
                act.wait_ge(um_evac, h + 1)
                act.nop().then_inc(ring.emptied["act"], 1)
                if h == 0:
                    ring.wait_filled(act, FA)
                    act.activation(dt, ring.bank(FA)[:, 2 * G2:3 * G2], ACT.Exp).then_inc(dt_ready, 1)
                    act.activation(ai, ring.bank(FA)[:, G2:2 * G2], ACT.Copy).then_inc(dt_ready, 1)
                    act.activation(ar, ring.bank(FA)[:, 0:G2], ACT.Copy).then_inc(dt_ready, 1)
                    act.wait_ge(dt_ready, 3)
                    act.nop().then_inc(ring.emptied["act"], 1)
                for jp in range(TC // 2):
                    ring.wait_filled(act, fu(h, jp))
                    copy(m.urow[:, :, 2 * jp:2 * jp + 2].rearrange("p g j c -> p j g c"),
                         ring.bank(fu(h, jp)).rearrange("p (j g c) -> p j g c", j=2, c=GC),
                         ring.emptied["act"])
                for q in range(4):
                    g = 16 * h + 4 * q
                    ring.wait_filled(act, ft(h, q))
                    copy(m.uj[:, g:g + 4, MCH:NCH], ring.bank(ft(h, q)).rearrange("p (g c) -> p g c", g=4),
                         ring.emptied["act"])
                ring.wait_filled(act, ftm(h))
                copy(m.uj[:, 16 * h:16 * h + 16, 0:MCH],
                     ring.bank(ftm(h))[:, 0:16 * MCH].rearrange("p (g c) -> p g c", g=16), ring.emptied["act"])
                if h == 0:
                    ring.wait_filled(act, FC)
                    act.activation(m.ca[:, 0, :, 0], ring.bank(FC)[:, 0:256].rearrange("p (g c) -> p g c", g=G2),
                                   ACT.Copy).then_inc(c_copied, 1)
                    act.activation(m.ca[:, 1, :, 0], ring.bank(FC)[:, 256:512].rearrange("p (g c) -> p g c", g=G2),
                                   ACT.Copy, scale=-1.0).then_inc(c_copied, 1)
                    act.wait_ge(c_copied, 2)
                    act.nop().then_inc(ring.emptied["act"], 1)
                    act.wait_ge(sq_ready, 1)
                    act.activation(m.radius, s1, ACT.Sqrt).then_inc(root_ready, 1)
            for q in range(8):
                ring.wait_filled(act, FW1 + q)
                copy(m.w1[:, 2 * q:2 * q + 2], ring.bank(FW1 + q).rearrange("p (g r s) -> p g r s", g=2, r=2),
                     ring.emptied["act"])
            act.wait_ge(zt_free, 1)
            for q in range(8):
                ring.wait_filled(act, FZ + q)
                copy(zt[:, 8 * (q // 2):8 * (q // 2) + 8, :].rearrange("p (i e) n -> p i e n", e=2)[:, :, q % 2], ring.bank(FZ + q)[0:GC, :].rearrange("p (g n) -> p g n", g=4),
                     ring.emptied["act"])

        @block.vector
        def _(dve):
            c = Chain(dve, steps)

            def tt(o, x, y, op):
                return dve.tensor_tensor(o, x, y, op)

            def cmul(ore, oim, xr, xi, yr, yi, t):
                tt(t[0], xr, yr, ALU.mult)
                tt(t[1], xi, yi, ALU.mult)
                tt(t[2], xr, yi, ALU.mult)
                c.link(tt(t[3], xi, yr, ALU.mult))
                tt(ore, t[0], t[1], ALU.subtract)
                c.link(tt(oim, t[2], t[3], ALU.add))

            dve.wait_ge(param_loaded, 48)
            dve.tensor_copy(arow[:, 2, :].rearrange("p (e n) -> p e n", e=2), bc(ldt, 2, NST)).then_inc(arow_ready, 1)
            dve.wait_ge(dt_ready, 3)
            c.link(dve.tensor_scalar(ar, ar, -1e-4, None, ALU.min))
            f = 2.0 ** -LOG_SCALE
            dve.scalar_tensor_tensor(zr, ar, f, dt, ALU.mult, ALU.mult)
            c.link(dve.scalar_tensor_tensor(zi, ai, f, dt, ALU.mult, ALU.mult))
            c.link(dve.tensor_scalar(er, zr, 1.0 / TAYLOR, 1.0, ALU.mult, ALU.add))
            c.link(dve.tensor_scalar(ei, zi, 1.0 / TAYLOR, None, ALU.mult))
            for d in range(TAYLOR - 1, 1, -1):
                cmul(s1, s2, zr, zi, er, ei, (s3, s4, s5, m.msq[:, 0:G2]))
                dve.tensor_scalar(er, s1, 1.0 / d, 1.0, ALU.mult, ALU.add)
                c.link(dve.tensor_scalar(ei, s2, 1.0 / d, None, ALU.mult))
            cmul(s1, s2, zr, zi, er, ei, (s3, s4, s5, m.msq[:, 0:G2]))
            cur, nxt = (s1, s2), (er, ei)
            for _ in range(LOG_SCALE):
                (xr, xi), (yr, yi) = cur, nxt
                dve.scalar_tensor_tensor(s3, xr, 2.0, xr, ALU.add, ALU.mult)
                tt(s4, xi, xi, ALU.mult)
                c.link(dve.scalar_tensor_tensor(s5, xr, 1.0, xi, ALU.add, ALU.mult))
                tt(yr, s3, s4, ALU.subtract)
                c.link(dve.tensor_scalar(yi, s5, 2.0, None, ALU.mult))
                cur, nxt = nxt, cur
            xr, xi = cur
            s6, s7 = nxt
            dve.memset(pw[:, 0, 0], 1.0)
            dve.memset(pw[:, 0, 1], 0.0)
            dve.tensor_scalar(pw[:, 1, 0], xr, 1.0, None, ALU.add)
            c.link(dve.tensor_copy(pw[:, 1, 1], xi))
            tmps = [t[:, 0:4 * G2].rearrange("p (k g) -> p k g", g=G2) for t in t4]
            for n in (1, 2, 4):
                cmul(pw[:, n + 1:2 * n + 1, 0], pw[:, n + 1:2 * n + 1, 1], pw[:, 1:n + 1, 0], pw[:, 1:n + 1, 1],
                     bc(pw[:, n, 0], 1, n), bc(pw[:, n, 1], 1, n), [t[:, 0:n] for t in tmps])
            dve.nop().then_inc(power_ready, 1)
            tt(s3, ar, ar, ALU.mult)
            c.link(tt(s4, ai, ai, ALU.mult))
            c.link(tt(s3, s3, s4, ALU.add))
            c.link(dve.reciprocal(s3, s3))
            tt(s4, xr, ar, ALU.mult)
            tt(s5, xi, ai, ALU.mult)
            tt(s6, xi, ar, ALU.mult)
            c.link(tt(s7, xr, ai, ALU.mult))
            tt(s4, s4, s5, ALU.add)
            c.link(tt(s6, s6, s7, ALU.subtract))
            tt(zr, s4, s3, ALU.mult)
            c.link(tt(zi, s6, s3, ALU.mult))
            a8r, a8i = pw[:, TC, 0], pw[:, TC, 1]
            tt(s2, a8r, a8r, ALU.mult)
            c.link(tt(s3, a8i, a8i, ALU.mult))
            c.link(tt(s2, s2, s3, ALU.add))
            dve.tensor_scalar(s1, s2, 1e-30, None, ALU.max).then_inc(sq_ready, 1)
            dve.wait_ge(b_loaded, 64)
            bb = [m.ba[:, r, :, TC - 1] for r in range(2)]
            tv = [t[:, 0:G2 * GC].rearrange("p (g c) -> p g c", g=G2) for t in t4]
            cmul(bb[0], bb[1], bc(zr, 2, GC), bc(zi, 2, GC), braw[:, 0], braw[:, 1], tv)
            for j in range(TC - 1):
                cmul(m.ba[:, 0, :, j], m.ba[:, 1, :, j], bc(pw[:, TC - 1 - j, 0], 2, GC), bc(pw[:, TC - 1 - j, 1], 2, GC),
                     bb[0], bb[1], tv)
            dve.nop().then_inc(ba_ready, 1)
            dve.wait_ge(root_ready, 1)
            c.link(dve.reciprocal(s3, m.radius))
            c.link(tt(s3, s3, s1, ALU.mult))
            c.link(tt(s3, s3, m.radius, ALU.add))
            c.link(dve.tensor_scalar(m.radius, s3, 0.5, None, ALU.mult))
            c.link(dve.reciprocal(s3, m.radius))
            dve.memset(m.turn[:, 0, :, 0], 1.0)
            dve.memset(m.turn[:, 1, :, 0], 0.0)
            tt(m.turn[:, 0, :, 1], a8r, s3, ALU.mult)
            c.link(tt(m.turn[:, 1, :, 1], a8i, s3, ALU.mult))
            n = 1
            while n + 1 < NCH:
                k = min(n, NCH - 1 - n)
                tv = [t[:, 0:G2 * k].rearrange("p (g c) -> p g c", g=G2) for t in t4]
                cmul(m.turn[:, 0, :, n + 1:n + 1 + k], m.turn[:, 1, :, n + 1:n + 1 + k],
                     m.turn[:, 0, :, 1:1 + k], m.turn[:, 1, :, 1:1 + k],
                     bc(m.turn[:, 0, :, n], 2, k), bc(m.turn[:, 1, :, n], 2, k), tv)
                n += k
            dve.nop().then_inc(zt_free, 1)
            dve.wait_ge(d_loaded, 16)
            dve.wait_ge(ring.emptied["act"], FZ + 8)
            diag = m.tmp[0:GC, 0:G * GC].rearrange("p (g c) -> p g c", g=G)
            c.link(tt(diag, bc(m.ident[0:GC, 0:GC], 1, G), bc(dcol, 2, GC), ALU.mult))
            tt(zt[:, :, 0:GC], zt[:, :, 0:GC], diag, ALU.add).then_inc(m.z_diag, 1)

        @block.gpsimd
        def _(pool):
            c = Chain(pool, ca_steps)
            pool.wait_ge(power_ready, 1)
            pool.wait_ge(ring.emptied["act"], FC + 1)
            cr, ci = m.ca[:, 0, :, 0], m.ca[:, 1, :, 0]
            tv = [t[:, 0:G2 * GC].rearrange("p (g c) -> p g c", g=G2) for t in pt]
            for k in range(1, TC + 1):
                pr, pi = bc(pw[:, k, 0], 2, GC), bc(pw[:, k, 1], 2, GC)
                pool.tensor_tensor(tv[0], cr, pr, ALU.mult)
                pool.tensor_tensor(tv[1], ci, pi, ALU.mult)
                pool.tensor_tensor(tv[2], ci, pr, ALU.mult)
                c.link(pool.tensor_tensor(tv[3], cr, pi, ALU.mult))
                pool.tensor_tensor(m.ca[:, 0, :, k], tv[0], tv[1], ALU.add)
                c.link(pool.tensor_tensor(m.ca[:, 1, :, k], tv[2], tv[3], ALU.subtract))
            pool.nop().then_inc(ca_ready, 1)
            pool.wait_ge(ring.emptied["act"], ftm(1) + 1)
            pool.memset(m.w3, 0.0).then_inc(m.w3_zero, 1)


def s5_stage(nc, m, a):
    yq = [m.urow.rearrange("p g j c -> p (g j c)")[:, 1024 * i:1024 * (i + 1)].rearrange("p (j n) -> p j n", j=TC)
          for i in range(2)]
    ymall = m.tmp[0:MCH, 0:1024].rearrange("p (j n) -> p j n", j=TC)
    w1flat = m.w1.rearrange("p g r s -> p (g r s)")
    ym = [w1flat[0:MCH, 1024 + 1024 * i:2048 + 1024 * i].rearrange("p (j n) -> p j n", j=TC) for i in range(2)]
    sg = [w1flat[:, 400 * i:400 * i + 400] for i in range(2)]
    tm = [m.tmp[:, 1008 * i:1008 * i + 910] for i in range(2)]

    by, index = [], {}

    def plan(key, who):
        index[key] = len(by)
        by.append(who)

    for g in range(G2):
        plan(("v", g), "act")
    gates = [("gs", 4)]
    for name, base in gates:
        for mt in range(4):
            for ch in range(3):
                plan(("gate", base + mt, ch), "act")

    def y_fills(kk):
        for q in range(2):
            plan(("y", kk, q), "act")
            plan(("ym", kk, q), "act")

    def t_fills(kk):
        for q in range(3):
            plan(("t", kk, q), "dve")

    order = [("y", 0), ("y", 1), ("t", 0), ("y", 2), ("t", 1), ("y", 3), ("t", 2), ("t", 3)]
    for what, kk in order:
        (y_fills if what == "y" else t_fills)(kk)
    for mt in range(4):
        for ch in range(3):
            plan(("glu", mt, ch), "act")
    ring = m.ring(m.banks, by)
    for name, base in gates:
        for half in range(2):
            m.section_end[f"{name}{half}"] = (ring.filled, index[("gate", base + 2 * half + 1, 2)] + 1)
    m.section_end["glu"] = (ring.filled, len(by))
    steps, states_ready, sg_used = (m.sem(x) for x in ("steps", "states_ready", "sg_used"))
    acount = lambda n: by[:n + 1].count("act")
    dcount = lambda n: by[:n + 1].count("dve")

    with nc.Block() as block:
        @block.sync
        def _(sp):
            sp.wait_ge(m.z_diag, 1)
            sp.wait_ge(m.w3_zero, 1)
            for j in range(TC):
                sp.dma_start(m.w3[GC * j:GC * j + GC, :, GC * j:P], m.zt[:, :, 0:P - GC * j]).then_inc(m.w3_moved, 16)
            send_sections(m, sp, m.section_at["q1"])

        @block.tensor
        def _(pe):
            def fill(key):
                n = index[key]
                ring.wait_free(pe, n)
                return ring.bank(n)

            for g2 in range(G2):
                b = fill(("v", g2))
                for e in range(2):
                    for r in range(2):
                        last = nc.tensor.matmul(b[NST * e:NST * e + NST, NCH * r:NCH * r + NCH],
                                                m.w1[:, g2, r, NST * e:NST * e + NST], m.uj[:, 2 * g2 + e, :],
                                                start=True, stop=True)
                last.then_inc(ring.filled, 1)
            for name, base in gates:
                for mt in range(4):
                    sec = f"{name}{mt // 2}"
                    w = section(m, sec)
                    if mt % 2 == 0:
                        wait_section(m, pe, sec)
                    for ch, (c0, c1) in enumerate(CHUNKS):
                        b = fill(("gate", base + mt, ch))
                        col_product(nc, m, pe, b[:, 0:c1 - c0],
                                    lambda k: w[:, k, P * (mt % 2):P * (mt % 2) + P],
                                    lambda k: m.xnT[:, k, c0:c1]).then_inc(ring.filled, 1)
            pe.wait_ge(states_ready, 1)
            pe.wait_ge(m.w3_moved, 16 * TC)
            for what, kk in order:
                if what == "y":
                    for q in range(2):
                        for meta in range(2):
                            b = fill(("ym" if meta else "y", kk, q))
                            cols = slice(0, MCH) if meta else slice(MCH, NCH)
                            n = MCH if meta else P
                            for i in range(4):
                                g = 8 * kk + 2 * i + q
                                rows = slice(NST * (g % 2), NST * (g % 2) + NST)
                                dst = b[0:n, P * i:P * i + P]
                                for r in range(2):
                                    nc.tensor.matmul(dst, m.v[rows, r, g // 2, cols], m.ca[rows, r, g // 2, 1:TC + 1],
                                                     start=(r == 0), stop=False)
                                last = nc.tensor.matmul(dst, m.uj[:, g, cols], m.w3[:, g, :], start=False, stop=True)
                            last.then_inc(ring.filled, 1)
                else:
                    n = index[("ym", kk, 1)]
                    pe.wait_ge(ring.emptied["act"], acount(n))
                    for q in range(2):
                        b = fill(("t", kk, q))
                        for i in range(4):
                            last = nc.tensor.transpose(b[:, P * i:P * i + P], yq[kk % 2][:, 4 * q + i, :], m.ident[:, :])
                        last.then_inc(ring.filled, 1)
                    b = fill(("t", kk, 2))
                    for j in range(TC):
                        last = nc.tensor.transpose(b[:, MCH * j:MCH * j + MCH], ym[kk % 2][:, j, :], m.ident[0:MCH, 0:MCH])
                    last.then_inc(ring.filled, 1)
            wait_section(m, pe, "glu")
            w = section(m, "glu")
            pe.wait_ge(ring.emptied["dve"], dcount(index[("t", 3, 2)]))
            for mt in range(4):
                for ch, (c0, c1) in enumerate(CHUNKS):
                    b = fill(("glu", mt, ch))
                    col_product(nc, m, pe, b[:, 0:c1 - c0], lambda k: w[:, k, P * mt:P * mt + P],
                                lambda k: m.yT[:, k, c0:c1], 4).then_inc(ring.filled, 1)

        @block.scalar
        def _(act):
            done = ring.emptied["act"]
            for g2 in range(G2):
                n = index[("v", g2)]
                ring.wait_filled(act, n)
                act.activation(m.v[:, :, g2, 1:NCH + 1], ring.bank(n)[:, 0:2 * NCH].rearrange("p (r c) -> p r c", r=2),
                               ACT.Copy).then_inc(done, 1)
            for name, base in gates:
                for mt in range(4):
                    for ch, (c0, c1) in enumerate(CHUNKS):
                        n = index[("gate", base + mt, ch)]
                        ring.wait_filled(act, n)
                        act.activation(m.mixT[:, base + mt, c0:c1], ring.bank(n)[:, 0:c1 - c0], ACT.Silu).then_inc(done, 1)
            for what, kk in order:
                if what != "y":
                    continue
                if kk >= 2:
                    act.wait_ge(ring.filled, index[("t", kk - 2, 2)] + 1)
                for q in range(2):
                    for key, dst, rows in (("y", yq, P), ("ym", ym, MCH)):
                        n = index[(key, kk, q)]
                        ring.wait_filled(act, n)
                        o = dst[kk % 2].rearrange("p j (g e c) -> p e g j c", e=2, c=GC)[:, q]
                        act.activation(o, ring.bank(n)[0:rows, :].rearrange("p (g j c) -> p g j c", g=4, j=TC),
                                       ACT.Gelu_apprx_tanh).then_inc(done, 1)
            i = 0
            for mt in range(4):
                for ch, (c0, c1) in enumerate(CHUNKS):
                    n = index[("glu", mt, ch)]
                    ring.wait_filled(act, n)
                    if i >= 2:
                        act.wait_ge(sg_used, i - 1)
                    act.activation(sg[i % 2][:, 0:c1 - c0], ring.bank(n)[:, 0:c1 - c0], ACT.Sigmoid,
                                   bias=m.bglu[:, mt:mt + 1]).then_inc(done, 1)
                    i += 1

        @block.vector
        def _(dve):
            c = Chain(dve, steps)

            def tt(o, x, y, op):
                return dve.tensor_tensor(o, x, y, op)

            c.link(dve.memset(m.v[:, :, :, 0], 0.0))
            parts = [(0, 7), (7, 14), (14, 16)]
            for g0, g1 in parts:
                n = g1 - g0
                dve.wait_ge(ring.emptied["act"], acount(index[("v", g1 - 1)]))
                vr, vi = m.v[:, 0, g0:g1, 1:NCH + 1], m.v[:, 1, g0:g1, 1:NCH + 1]
                pr, pi = m.turn[:, 0, g0:g1, :], m.turn[:, 1, g0:g1, :]
                t0, t1 = (t[:, 0:n * NCH].rearrange("p (g c) -> p g c", g=n) for t in tm)
                tt(t0, vr, pr, ALU.mult)
                c.link(tt(t1, vr, pi, ALU.mult))
                tt(vr, vi, pi, ALU.mult)
                c.link(tt(vi, vi, pr, ALU.mult))
                tt(vr, vr, t0, ALU.add)
                c.link(tt(vi, vi, t1, ALU.subtract))
                for g in range(g0, g1):
                    for r in range(2):
                        row = m.v[:, r, g, 1:NCH + 1]
                        ins = dve.tensor_tensor_scan(row, m.radius[:, g:g + 1].broadcast_to((P, NCH)), row, 0.0,
                                                     ALU.mult, ALU.add)
                c.link(ins)
                tt(t0, vr, pr, ALU.mult)
                c.link(tt(t1, vr, pi, ALU.mult))
                tt(vr, vi, pi, ALU.mult)
                c.link(tt(vi, vi, pr, ALU.mult))
                dve.tensor_tensor(vr, t0, vr, ALU.subtract)
                c.link(tt(vi, vi, t1, ALU.add))
            dve.nop().then_inc(states_ready, 1)
            for kk in range(4):
                frames = m.yT[:, kk, META:L].rearrange("p (c j) -> p j c", j=TC)
                for q in range(2):
                    n = index[("t", kk, q)]
                    ring.wait_filled(dve, n)
                    dve.tensor_copy(frames[:, 4 * q:4 * q + 4], ring.bank(n).rearrange("p (j c) -> p j c", j=4)
                                    ).then_inc(ring.emptied["dve"], 1)
                n = index[("t", kk, 2)]
                ring.wait_filled(dve, n)
                dve.tensor_copy(m.yT[:, kk, 0:META].rearrange("p (c j) -> p j c", j=TC),
                                ring.bank(n)[:, 0:META].rearrange("p (j c) -> p j c", j=TC)
                                ).then_inc(ring.emptied["dve"], 1)
            dve.wait_ge(ring.emptied["dve"], by.count("dve"))
            i = 0
            for mt in range(4):
                for ch, (c0, c1) in enumerate(CHUNKS):
                    dve.wait_ge(ring.emptied["act"], acount(index[("glu", mt, ch)]))
                    s = sg[i % 2][:, 0:c1 - c0]
                    c.link(tt(s, s, m.yT[:, mt, c0:c1], ALU.mult))
                    g = m.mixT[:, 4 + mt, c0:c1]
                    tt(g, g, s, ALU.mult).then_inc(sg_used, 1)
                    i += 1


def feature_stage(nc, m, area, tiles, sources, upto):
    zt = [area.take(f"z{i}_{upto}", L) for i in range(2)]
    sq = [area.take(f"squares{i}_{upto}", L) for i in range(2)]
    rs = area.take(f"root_{upto}", L)
    NM = len(tiles)
    by, index = [], {}

    def plan(key, who):
        index[key] = len(by)
        by.append(who)

    for i in range(NM + 2):
        if i < NM:
            for c in range(len(tiles[i]["chunks"])):
                plan(("mm", i, c), "act")
        if 0 <= i - 1 < NM:
            t = tiles[i - 1]
            if t["kind"] == "n":
                for c in range(len(t["chunks"])):
                    plan(("ms", i - 1, c), "act")
            elif t["kind"] == "r":
                for c in range(3):
                    plan(("tr", i - 1, c), "dve")
        if 0 <= i - 2 < NM and "dup" in tiles[i - 2]:
            for v in range(2):
                for c in range(3):
                    plan(("dup", i - 2, v, c), "dve")
    ring = m.ring(m.banks, by)
    normal = [i for i in range(NM) if tiles[i]["kind"] == "n"]
    w_hi, w_lo, w_first_hi, w_first, squared, copied, rooted, inverted, finished = (
        m.sem(x) for x in ("w_hi", "w_lo", "w_first_hi", "w_first", "squared", "copied", "rooted", "inverted", "finished"))
    xs = [m.sem(x) for x in ("x_hi_act", "x_hi_dve", "x_lo_pool", "x_lo_dve")]
    for i, t in enumerate(tiles):
        m.section_end[t["section"]] = (w_lo, i) if i >= 2 else (ring.filled, index[("mm", i, 2)] + 1)
    acount = lambda n: by[:n + 1].count("act")

    def raw_weights(i):
        t = tiles[i]
        return section(m, t["section"])[:, :, P * t["half"]:P * t["half"] + P]

    with nc.Block() as block:
        @block.sync
        def _(sp):
            send_sections(m, sp, upto)

        @block.tensor
        def _(pe):
            for i in range(NM + 2):
                if i < NM:
                    t = tiles[i]
                    if i == 0:
                        pe.wait_ge(w_first, 1)
                    else:
                        pe.wait_ge(w_lo, i)
                    for c, (c0, c1) in enumerate(t["chunks"]):
                        n = index[("mm", i, c)]
                        ring.wait_free(pe, n)
                        before = (lambda k: wait_split(pe, k, xs, c1)) if i == 0 else None
                        split_product(nc, ring.bank(n)[:, 0:c1 - c0], lambda k: (m.whi[i % 2][:, k], m.wlo[i % 2][:, k]),
                                      lambda k: (m.xhi[:, k, c0:c1], m.xlo[:, k, c0:c1]), before=before
                                      ).then_inc(ring.filled, 1)
                if 0 <= i - 1 < NM:
                    t = tiles[i - 1]
                    if t["kind"] == "n":
                        for c, (c0, c1) in enumerate(t["chunks"]):
                            n = index[("ms", i - 1, c)]
                            ring.wait_free(pe, n)
                            pe.wait_ge(ring.emptied["act"], acount(index[("mm", i - 1, c)]))
                            nc.tensor.matmul(ring.bank(n)[:, 0:c1 - c0], m.headmean[:, :], sq[(i - 1) % 2][:, c0:c1],
                                             start=True, stop=True).then_inc(ring.filled, 1)
                    elif t["kind"] == "r":
                        pe.wait_ge(ring.emptied["act"], acount(index[("mm", i - 1, 2)]))
                        z = zt[(i - 1) % 2]
                        for c in range(3):
                            n = index[("tr", i - 1, c)]
                            ring.wait_free(pe, n)
                            if c == 2:
                                last = nc.tensor.transpose(ring.bank(n)[0:META, 0:P], z[:, 0:META], m.ident[:, :])
                            else:
                                for b in range(4):
                                    c0 = META + P * (4 * c + b)
                                    last = nc.tensor.transpose(ring.bank(n)[:, P * b:P * b + P], z[:, c0:c0 + P], m.ident[:, :])
                            last.then_inc(ring.filled, 1)
                if 0 <= i - 2 < NM and "dup" in tiles[i - 2]:
                    t = tiles[i - 2]
                    pe.wait_ge(finished, normal.index(i - 2) + 1)
                    for v in range(2):
                        for c, (c0, c1) in enumerate(CHUNKS):
                            n = index[("dup", i - 2, v, c)]
                            ring.wait_free(pe, n)
                            nc.tensor.matmul(ring.bank(n)[:, 0:c1 - c0], m.kvcopy[:, P * v:P * v + P], t["dst"](c0, c1),
                                             start=True, stop=True).then_inc(ring.filled, 1)

        @block.scalar
        def _(act):
            split_tiles(act, None, None, sources, m.xhi, m.xlo, xs)

            def round_weights(i):
                if i == 0 or i >= NM:
                    return
                if i >= 2:
                    act.wait_ge(ring.filled, index[("mm", i - 2, len(tiles[i - 2]["chunks"]) - 1)] + 1)
                wait_section(m, act, tiles[i]["section"])
                act.activation(m.whi[i % 2], raw_weights(i), ACT.Copy).then_inc(w_hi, 1)

            for i in range(NM + 1):
                if i < NM:
                    t = tiles[i]
                    round_weights(i + 1)
                    if t["kind"] in "nr" and i >= 2:
                        p = tiles[i - 2]
                        if p["kind"] == "n":
                            act.wait_ge(finished, normal.index(i - 2) + 1)
                        elif p["kind"] == "r":
                            act.wait_ge(ring.filled, index[("tr", i - 2, 2)] + 1)
                    for c, (c0, c1) in enumerate(t["chunks"]):
                        n = index[("mm", i, c)]
                        ring.wait_filled(act, n)
                        z = ring.bank(n)[:, 0:c1 - c0]
                        if t["kind"] == "n":
                            act.activation(zt[i % 2][:, c0:c1], z, ACT.Copy).then_inc(copied, 1)
                            act.activation(sq[i % 2][:, c0:c1], z, ACT.Square).then_inc(ring.emptied["act"], 1)
                        elif t["kind"] == "r":
                            act.activation(zt[i % 2][:, c0:c1], z, ACT.Copy).then_inc(ring.emptied["act"], 1)
                        else:
                            act.activation(t["dst"](c0, c1), z, ACT.Silu if t["kind"] == "g" else ACT.Copy
                                           ).then_inc(ring.emptied["act"], 1)
                if 0 <= i - 1 and tiles[i - 1]["kind"] == "n":
                    k = normal.index(i - 1)
                    if k >= 1:
                        act.wait_ge(finished, k)
                    for c, (c0, c1) in enumerate(tiles[i - 1]["chunks"]):
                        n = index[("ms", i - 1, c)]
                        ring.wait_filled(act, n)
                        act.activation(rs[:, c0:c1], ring.bank(n)[:, 0:c1 - c0], ACT.Sqrt, bias=m.eps
                                       ).then_inc(ring.emptied["act"], 1)

        @block.gpsimd
        def _(pool):
            split_tiles(None, None, pool, sources, m.xhi, m.xlo, xs)
            for i in range(1, NM):
                pool.wait_ge(w_hi, i)
                if i >= 2:
                    pool.wait_ge(ring.filled, index[("mm", i - 2, len(tiles[i - 2]["chunks"]) - 1)] + 1)
                pool.tensor_tensor(m.wlo[i % 2], raw_weights(i), m.whi[i % 2].bitcast(F32), ALU.subtract).then_inc(w_lo, 1)

        @block.vector
        def _(dve):
            wait_section(m, dve, tiles[0]["section"])
            dve.tensor_copy(m.whi[0], raw_weights(0)).then_inc(w_first_hi, 1)
            dve.wait_ge(w_first_hi, 1)
            dve.tensor_tensor(m.wlo[0], raw_weights(0), m.whi[0].bitcast(F32), ALU.subtract).then_inc(w_first, 1)
            split_tiles(None, dve, None, sources, m.xhi, m.xlo, xs)
            for i in range(1, NM + 2):
                if 0 <= i - 1 < NM:
                    t = tiles[i - 1]
                    if t["kind"] == "n":
                        k = normal.index(i - 1)
                        c0, c1 = t["chunks"][0][0], t["chunks"][-1][1]
                        dve.wait_ge(ring.emptied["act"], acount(index[("ms", i - 1, len(t["chunks"]) - 1)]))
                        dve.reciprocal(rs[:, c0:c1], rs[:, c0:c1]).then_inc(inverted, 1)
                        dve.wait_ge(inverted, k + 1)
                        dve.scalar_tensor_tensor(t["dst"](c0, c1), zt[(i - 1) % 2][:, c0:c1], t["gain"], rs[:, c0:c1],
                                                 ALU.mult, ALU.mult).then_inc(finished, 1)
                    elif t["kind"] == "r":
                        for c in range(3):
                            n = index[("tr", i - 1, c)]
                            ring.wait_filled(dve, n)
                            if c == 2:
                                dst, src = t["rows"](0, 1)[0:META, 0], ring.bank(n)[0:META, 0:P]
                            else:
                                dst, src = t["rows"](1 + 4 * c, 5 + 4 * c), ring.bank(n).rearrange("p (t n) -> p t n", t=4)
                            dve.tensor_copy(dst, src).then_inc(ring.emptied["dve"], 1)
                if 0 <= i - 2 and "dup" in tiles[i - 2]:
                    for v in range(2):
                        for c, (c0, c1) in enumerate(CHUNKS):
                            n = index[("dup", i - 2, v, c)]
                            ring.wait_filled(dve, n)
                            dve.tensor_copy(tiles[i - 2]["dup"][:, v, c0:c1], ring.bank(n)[:, 0:c1 - c0]
                                            ).then_inc(ring.emptied["dve"], 1)


def qkv_stage(nc, m, a, area):
    m.qT = m.qk[:, 0:4 * L].rearrange("p (k l) -> p k l", k=4)
    m.kT = m.qk[:, 4 * L:8 * L].rearrange("p (k l) -> p k l", k=4)
    m.vrow = m.vrows.rearrange("p (t n) -> p t n", t=NT)
    tiles = []
    for side, dst in (("q", m.qT), ("k", m.kT)):
        for p in range(NPAIR):
            tiles.append(dict(kind="n", section=f"{side}{p // 2}", half=p % 2, chunks=CHUNKS, gain=m.head_gain["ev" + side],
                              dst=lambda c0, c1, d=dst, p=p: d[:, p, c0:c1]))
    for p in range(NPAIR):
        tiles.append(dict(kind="r", section=f"v{p // 2}", half=p % 2, chunks=CHUNKS,
                          rows=lambda t0, t1, p=p: m.vrow[:, t0:t1, P * p:P * p + P]))
    for p in range(NPAIR):
        tiles.append(dict(kind="g", section=f"gb{p // 2}", half=p % 2, chunks=CHUNKS,
                          dst=lambda c0, c1, p=p: m.mixT[:, p, c0:c1]))
    feature_stage(nc, m, area, tiles, m.xnT, m.section_at["eo1"])


def stick_breaking_stage(nc, m, a, area):
    def take(name, slots, dt=F32):
        return [area.take(f"{name}{i}", BANK, dt) for i in range(slots)]

    lg, soft, wt, total = take("log", NLOG), take("softplus", NSOFT), take("weights", NWEIGHT), take("total", NTOTAL)
    sp_hi, sp_lo = (take(x, NSPLIT, F32R) for x in ("softplus_hi", "softplus_lo"))
    tri = area.take("tri_r", P, F32R)

    its, finals = [], []
    for p in range(NPAIR):
        for c0, c1 in QUERIES:
            blocks = [b for b in range(NT) if tile_cols(b)[0] < c1]
            for b in reversed(blocks):
                k0, kn = tile_cols(b)
                q0 = max(c0, k0)
                for h in range(2):
                    its.append(dict(p=p, h=h, b=b, k0=k0, kn=kn, q0=q0, q1=c1, c0=c0, n=c1 - q0,
                                    diag=k0 >= c0, first=b == blocks[-1], last=b == 0, acc=len(finals)))
            finals.append((p, c0, c1, len(its) - 1))
    NI = len(its)
    z = m.banks[0:NZ]
    acc = [b[:, :] for b in m.bank]
    scored, capped, exped, logged, softened, sp_rounded, sp_split = (m.sem(x) for x in (
        "scored", "capped", "exped", "logged", "softened", "sp_rounded", "sp_split"))
    totalled, extended = m.sem("totalled"), m.sem("extended")
    summed, weighted, weighed, finished, tri_ready, capped_dve = (m.sem(x) for x in (
        "summed", "weighted", "weighed", "finished", "tri_ready", "capped_dve"))

    def totals(i):
        return sum(1 for t in its[:i + 1] if not t["last"])

    def capped_by_dve(i):
        return 0 < i < NI and i % DVE_CAPS_EVERY == 0

    def caps_dve(i):
        return sum(1 for k in range(i + 1) if capped_by_dve(k))

    steps_with_total = [i for i, t in enumerate(its) if not t["last"]]

    with nc.Block() as block:
        @block.tensor
        def _(pe):
            def score(i):
                t = its[i]
                r, kn, n = slice(HD * t["h"], HD * t["h"] + HD), t["kn"], t["n"]
                if i >= NZ:
                    pe.wait_ge(weighted, i - NZ + 1)
                last = nc.tensor.matmul(z[i % NZ][0:kn, 0:n], m.kT[r, t["p"], t["k0"]:t["k0"] + kn],
                                        m.qT[r, t["p"], t["q0"]:t["q1"]], start=True, stop=not t["diag"])
                if t["diag"]:
                    last = nc.tensor.matmul(z[i % NZ][0:kn, 0:kn], m.identb[0:kn, 0:kn], m.negmask[0:kn, 0:kn],
                                            start=False, stop=True)
                last.then_inc(scored, 1)

            def take_sums(i):
                t = its[i]
                kn, n = t["kn"], t["n"]
                pe.wait_ge(sp_split, i + 1)
                for part in (sp_hi, sp_lo):
                    last = nc.tensor.matmul(z[i % NZ][0:kn, 0:n], tri[0:kn, 0:kn], part[i % NSPLIT][0:kn, 0:n],
                                            start=False, stop=True, skip_group_check=True)
                if not t["first"]:
                    before = its[i - 2]["q0"]
                    dst, cols = z[i % NZ][0:kn, before - t["q0"]:n], slice(before - t["c0"], t["q1"] - t["c0"])
                    j = totals(i - 2)
                    pe.wait_ge(totalled, j)
                    last = nc.tensor.matmul(dst, m.ones[:, 0:kn], total[j % NTOTAL][:, cols],
                                            start=False, stop=True, skip_group_check=True)
                last.then_inc(summed, 1)

            def weigh(i):
                t = its[i]
                pe.wait_ge(weighted, i + 1)
                if t["first"] and t["acc"] >= 2:
                    pe.wait_ge(finished, t["acc"] - 1)
                hh = 2 * t["p"] + t["h"]
                r = slice(HD * t["h"], HD * t["h"] + HD)
                nc.tensor.matmul(acc[t["acc"] % 2][r, t["q0"] - t["c0"]:t["q1"] - t["c0"]],
                                 m.vrow[0:t["kn"], t["b"], HD * hh:HD * hh + HD], wt[i % NWEIGHT][0:t["kn"], 0:t["n"]],
                                 start=t["first"], stop=t["last"], skip_group_check=True).then_inc(weighed, 1)

            pe.wait_ge(tri_ready, 1)
            for i in range(NI + LAG + 1):
                if i < NI:
                    score(i)
                if 0 <= i - LAG < NI:
                    take_sums(i - LAG)
                if 0 <= i - LAG - 1 < NI:
                    weigh(i - LAG - 1)

        @block.scalar
        def _(act):
            act.preload_act_table_set("natural_log_exp_and_others")

            def weights(i):
                t = its[i]
                here = slice(0, t["kn"]), slice(0, t["n"])
                act.wait_ge(summed, i + 1)
                if i >= NWEIGHT:
                    act.wait_ge(weighed, i - NWEIGHT + 1)
                act.activation(wt[i % NWEIGHT][here], z[i % NZ][here], ACT.Exp).then_inc(weighted, 1)

            for i in range(NI + LAG):
                if 0 <= i - LAG < NI:
                    weights(i - LAG)
                if i < NI:
                    t = its[i]
                    here = slice(0, t["kn"]), slice(0, t["n"])
                    v = lg[i % NLOG][here]
                    if capped_by_dve(i):
                        act.wait_ge(capped_dve, caps_dve(i))
                    else:
                        act.wait_ge(scored, i + 1)
                        if i >= NLOG:
                            act.wait_ge(softened, i - NLOG + 1)
                        act.activation(v, z[i % NZ][here], ACT.Abs).then_inc(capped, 1)
                        act.wait_ge(capped, i + 1 - caps_dve(i))
                    act.activation(v, v, ACT.Exp, scale=-1.0).then_inc(exped, 1)
                    act.wait_ge(exped, i + 1)
                    act.activation(v, v, ACT.Ln, bias=1.0).then_inc(logged, 1)

        @block.vector
        def _(dve):
            ends = {last: n for n, (_, _, _, last) in enumerate(finals)}

            def finish(n):
                p, c0, c1, last = finals[n]
                dve.wait_ge(weighed, last + 1)
                g = m.mixT[:, p, c0:c1]
                dve.tensor_tensor(g, g, acc[n % 2][:, 0:c1 - c0], ALU.mult).then_inc(finished, 1)

            dve.tensor_copy(tri, m.tri[:, :]).then_inc(tri_ready, 1)
            for i in range(NI + LAG + 3):
                if capped_by_dve(i + 1):
                    t = its[i + 1]
                    here = slice(0, t["kn"]), slice(0, t["n"])
                    dve.wait_ge(scored, i + 2)
                    if i + 1 >= NLOG:
                        dve.wait_ge(softened, i - NLOG + 2)
                    dve.tensor_scalar(lg[(i + 1) % NLOG][here].bitcast(I32), z[(i + 1) % NZ][here].bitcast(I32),
                                      0x7FFFFFFF, None, ALU.bitwise_and).then_inc(capped_dve, 1)
                if i < NI:
                    t = its[i]
                    here = slice(0, t["kn"]), slice(0, t["n"])
                    s, hi = soft[i % NSOFT][here], sp_hi[i % NSPLIT][here]
                    dve.wait_ge(logged, i + 1)
                    if i >= NSOFT:
                        dve.wait_ge(totalled, totals(i - NSOFT))
                        dve.wait_ge(sp_split, i - NSOFT + 1)
                    dve.scalar_tensor_tensor(s, z[i % NZ][here], 0.0, lg[i % NLOG][here], ALU.max, ALU.add).then_inc(softened, 1)
                    dve.wait_ge(softened, i + 1)
                    if i >= NSPLIT:
                        dve.wait_ge(summed, i - NSPLIT + 1)
                    dve.tensor_copy(hi, s).then_inc(sp_rounded, 1)
                    dve.wait_ge(sp_rounded, i + 1)
                    dve.tensor_tensor(sp_lo[i % NSPLIT][here], s, hi.bitcast(F32), ALU.subtract).then_inc(sp_split, 1)
                if i - LAG - 2 in ends:
                    finish(ends[i - LAG - 2])

        @block.gpsimd
        def _(pool):
            for i in steps_with_total:
                t, n = its[i], totals(i)
                pool.wait_ge(softened, i + 1)
                if n >= 3:
                    pool.wait_ge(totalled, n - 2)
                if n > NTOTAL:
                    pool.wait_ge(summed, steps_with_total[n - NTOTAL - 1] + 3)
                q0, q1 = t["q0"] - t["c0"], t["q1"] - t["c0"]
                s, dst, src = soft[i % NSOFT], total[n % NTOTAL], total[(n - 2) % NTOTAL]
                if t["first"]:
                    pool.tensor_copy(dst[:, q0:q1], s[:, 0:t["n"]]).then_inc(totalled, 1)
                else:
                    o = its[i - 2]["q0"] - t["c0"]
                    if o > q0:
                        pool.tensor_copy(dst[:, q0:o], s[:, 0:o - q0]).then_inc(extended, 1)
                    pool.tensor_tensor(dst[:, o:q1], src[:, o:q1], s[:, o - q0:t["n"]], ALU.add).then_inc(totalled, 1)


def split_mix(m, area, layer):
    src = m.mixT
    m.mlo = m.mixlo.rearrange("p (k l) -> p k l", k=KD)
    m.mhi = area.take(f"mix_hi{layer}", 8 * L, F32R).rearrange("p (k l) -> p k l", k=KD)
    return src


def out_weights(area, layer):
    return [[area.take(f"wo_{part}{layer}{i}", KD * SEC, F32R).rearrange("p (k n) -> p k n", k=KD) for i in range(2)]
            for part in ("hi", "lo")]


def out_split_engines(m, act, dve, pool, src, names, whi, wlo, xs, ws, free, first=0):
    w_hi, w_lo, w_first_hi, w_first = ws
    if act:
        split_tiles(act, None, None, src, m.mhi, m.mlo, xs, first)
    if dve:
        wait_section(m, dve, names[0])
        raw = section(m, names[0])
        dve.tensor_copy(whi[0], raw).then_inc(w_first_hi, 1)
        dve.wait_ge(w_first_hi, 1)
        dve.tensor_tensor(wlo[0], raw, whi[0].bitcast(F32), ALU.subtract).then_inc(w_first, 1)
        split_tiles(None, dve, None, src, m.mhi, m.mlo, xs, first)
    if pool:
        split_tiles(None, None, pool, src, m.mhi, m.mlo, xs, first)
    if act:
        for n in range(1, 4):
            if n >= 2:
                act.wait_ge(*free(n - 2))
            wait_section(m, act, names[n])
            act.activation(whi[n % 2], section(m, names[n]), ACT.Copy).then_inc(w_hi, 1)
    if pool:
        for n in range(1, 4):
            pool.wait_ge(w_hi, n)
            if n >= 2:
                pool.wait_ge(*free(n - 2))
            pool.tensor_tensor(wlo[n % 2], section(m, names[n]), whi[n % 2].bitcast(F32), ALU.subtract).then_inc(w_lo, 1)


def out_product(nc, m, pe, ring, i, cols, n, rows, whi, wlo, xs, ws):
    ring.wait_free(pe, i)
    before = (lambda k: wait_split(pe, k, xs, cols.stop)) if n == 0 else None
    split_product(nc, ring.bank(i)[0:rows, 0:SEC], lambda k: (m.mhi[:, k, cols], m.mlo[:, k, cols]),
                  lambda k: (whi[n % 2][:, k], wlo[n % 2][:, k]), before=before).then_inc(ring.filled, 1)


def wait_out_weights(pe, ws, n):
    if n == 0:
        pe.wait_ge(ws[3], 1)
    else:
        pe.wait_ge(ws[1], n)


def even_out_stage(nc, m, a, area):
    f = area.take("h1_rows", HEAD)
    m.xn = area.take("xn1", KD * L)
    m.xnT = m.xn.rearrange("p (k l) -> p k l", k=KD)
    src = split_mix(m, area, 0)
    whi, wlo = out_weights(area, 0)
    h1 = f[:, 0:NT * D].rearrange("p (t n) -> p t n", t=NT)
    xs_ = [f[:, NT * D + D * i:NT * D + D * (i + 1)] for i in range(2)]
    junk = f[:, NT * D + 2 * D:NT * D + 3 * D]
    m.h1_dram = nc.dram_tensor("h1_frames", (SEQ, D), F32, kind="Internal").ap()
    m.h1_stored = m.sem("h1_stored")
    row_loaded = [m.sem("row_loaded") for _ in range(3)]
    names = [f"eo{n}" for n in range(4)]
    by, index = [], {}

    def plan(key, who):
        index[key] = len(by)
        by.append(who)

    for n in range(3):
        for t in range(NT):
            plan(("mm", n, t), "dve")
    for t in range(NT + 2):
        if t < NT:
            plan(("mm", 3, t), "dve")
        if t >= 2:
            for h in range(2):
                plan(("tr", t - 2, h), "dve")
    ring = m.ring(m.banks, by)
    xs = [m.sem(x) for x in ("mix_hi_act", "mix_hi_dve", "mix_lo_pool", "mix_lo_dve")]
    ws = [m.sem(x) for x in ("w_hi", "w_lo", "w_first_hi", "w_first")]
    for n in range(4):
        m.section_end[names[n]] = (ws[1], n) if n else (ws[3], 1)
    free = lambda n: (ring.filled, index[("mm", n, NT - 1)] + 1)
    sq_done, ms_done, rt_done, rs_done, scaled = (m.sem(x) for x in ("sq_done", "ms_done", "rt_done", "rs_done", "scaled"))
    dcount = lambda n: by[:n + 1].count("dve")

    with nc.Block() as block:
        @block.sync
        def _(sp):
            sp.dma_start(h1[0:META, 0, :], a["meta_tokens"]).then_inc(row_loaded[0], 16)
            for h in range(2):
                sp.dma_start(h1[:, 1 + 4 * h:5 + 4 * h, :], a["x"][0, 512 * h:512 * h + 512, :]
                             .rearrange("(t p) n -> p t n", p=P)).then_inc(row_loaded[1 + h], 16)
            send_sections(m, sp, m.section_at["oq0"])
            for t in range(1, NT):
                sp.wait_ge(ring.emptied["dve"], dcount(index[("mm", 3, t)]))
                sp.dma_start(m.h1_dram[P * (t - 1):P * t, :], h1[:, t, :]).then_inc(m.h1_stored, 16)
            sp.wait_ge(m.h1_stored, 16 * (NT - 1))

        @block.tensor
        def _(pe):
            def product(n, t):
                c0, rows = tile_cols(t)
                if t == 0:
                    wait_out_weights(pe, ws, n)
                out_product(nc, m, pe, ring, index[("mm", n, t)], slice(c0, c0 + rows), n, rows, whi, wlo, xs, ws)

            for n in range(3):
                for t in range(NT):
                    product(n, t)
            for t in range(NT + 2):
                if t < NT:
                    product(3, t)
                if t >= 2:
                    pe.wait_ge(scaled, t - 1)
                    for h in range(2):
                        transpose_half(nc, m, pe, ring, index[("tr", t - 2, h)], xs_[t % 2], tile_cols(t - 2)[1], h)

        @block.vector
        def _(dve):
            out_split_engines(m, None, dve, None, src, names, whi, wlo, xs, ws, free)

            def add(n, t):
                rows = tile_cols(t)[1]
                i = index[("mm", n, t)]
                ring.wait_filled(dve, i)
                x = h1[0:rows, t, SEC * n:SEC * n + SEC]
                dve.tensor_tensor(x, x, ring.bank(i)[0:rows, 0:SEC], ALU.add).then_inc(ring.emptied["dve"], 1)

            for n in range(3):
                for t in range(NT):
                    if n == 0 and t in (0, 1, 5):
                        dve.wait_ge(row_loaded[(t + 3) // 4], 16)
                    add(n, t)
            for t in range(NT + 2):
                if t < NT:
                    add(3, t)
                    rstd_steps(dve, m, t, tile_cols(t)[1], sq_done, ms_done, rt_done, rs_done)
                if t >= 2:
                    empty_transposes(dve, m, ring, index[("tr", t - 2, 0)], t - 2, "od")

        @block.scalar
        def _(act):
            out_split_engines(m, act, None, None, src, names, whi, wlo, xs, ws, free)
            for t in range(NT):
                n = tile_cols(t)[1]
                act.wait_ge(ring.emptied["dve"], dcount(index[("mm", 3, t)]))
                act.activation(junk[0:n, :], h1[0:n, t, :], ACT.Square, accum_out=m.ss[0:n, t:t + 1]).then_inc(sq_done, 1)
                act.wait_ge(ms_done, t + 1)
                act.activation(m.rstd[0:n, t:t + 1], m.msq[0:n, t:t + 1], ACT.Sqrt).then_inc(rt_done, 1)
                act.wait_ge(rs_done, t + 1)
                if t >= 2:
                    act.wait_ge(ring.filled, index[("tr", t - 2, 1)] + 1)
                act.activation(xs_[t % 2][0:n, :], h1[0:n, t, :], ACT.Copy, scale=m.rstd[0:n, t:t + 1]).then_inc(scaled, 1)

        @block.gpsimd
        def _(pool):
            out_split_engines(m, None, None, pool, src, names, whi, wlo, xs, ws, free)


BAND = 3 * HD
NKEY = BAND + META


def odd_in_stage(nc, m, a, area):
    f = m.qkv1
    m.q1T = f[:, 0:8 * SEQ].rearrange("p (k l) -> p k l", k=8)
    m.k1T = f[:, 8192:8192 + 2 * L].rearrange("p (k l) -> p k l", k=2)
    m.v1T = f[:, 8192 + 2 * L:8192 + 3 * L]
    both = f[:, 8192 + 3 * L:8192 + 4 * L]
    frames = [(META, META + 512), (META + 512, L)]
    tiles = [dict(kind="n", section="okv", half=0, chunks=CHUNKS, gain=m.head_gain["odk"], dup=m.k1T,
                  dst=lambda c0, c1: both[:, c0:c1]),
             dict(kind="c", section="okv", half=1, chunks=CHUNKS, dst=lambda c0, c1: m.v1T[:, c0:c1])]
    for p in range(8):
        tiles.append(dict(kind="n", section=f"oq{p // 2}", half=p % 2, chunks=frames, gain=m.head_gain["odq"],
                          dst=lambda c0, c1, p=p: m.q1T[:, p, c0 - META:c1 - META]))
    for p in range(8):
        tiles.append(dict(kind="g", section=f"og{p // 2}", half=p % 2, chunks=frames,
                          dst=lambda c0, c1, p=p: m.mixT[:, p, c0:c1]))
    feature_stage(nc, m, area, tiles, m.xnT, m.section_at["oo1"])


def window_stage(nc, m, a, area):
    NQ = NT - 1
    NH, HG = 16, 4
    bias_hi, bias_lo = (area.take(x, NH * NKEY, F32R).rearrange("p (h n) -> p h n", h=NH) for x in ("bias_hi", "bias_lo"))
    ident = area.take("ident_r", P, F32R)
    kb = area.take("key_band", 2 * NQ * NKEY).rearrange("p (v i n) -> p v i n", v=2, i=NQ)
    vb = area.take("value_band", NQ * NKEY).rearrange("p (i n) -> p i n", i=NQ)
    dist = area.take("dist", NKEY)
    idist = area.take("idist", BAND).bitcast(I32)
    pbuf = [area.take(f"probs{i}", HG * NKEY).rearrange("p (h n) -> p h n", h=HG) for i in range(4)]
    v_hi, v_lo = (area.take(x, NQ * 2 * P, F32R).rearrange("p (i b n) -> p i b n", i=NQ, b=2) for x in ("v_hi", "v_lo"))
    pt_hi, pt_lo = ([area.take(f"{x}{i}", 2 * BANK, F32R).rearrange("p (b n) -> p b n", b=2) for i in range(2)]
                    for x in ("probs_hi", "probs_lo"))
    NB = NKEY - P
    slots = [dict(nm=m.small(HG), den=m.small(HG), es=m.small(HG), mx=m.small(HG)) for _ in range(4)]

    def place(j):
        return 2 * (j % 2) + j // 2

    its = [(i, hg) for i in range(NQ) for hg in range(NH // HG)]
    NI = len(its)
    iota_done, steps, vb_ready, vt_filled, v_rounded, v_split = (
        m.sem(x) for x in ("iota_done", "steps", "vb_ready", "vt_filled", "v_rounded", "v_split"))
    scored, bias_rounded, bias_split, maxed, exped, sink_exped, inverted, normed, turned, pt_rounded, pt_split, weighed, gated = (
        m.sem(x) for x in ("scored", "bias_rounded", "bias_split", "maxed", "exped", "sink_exped", "inverted", "normed", "turned",
                           "pt_rounded", "pt_split", "weighed", "gated"))
    sc = [m.wide[0], m.wide[1]]
    pta, ptb_ps = m.wide[2][:, 0:BANK], m.wide[2][:, BANK:2 * BANK]
    pt = ((pta, P), (ptb_ps, NB))

    def v_rows(i):
        return m.banks[4 + i].rearrange("p (t b n) -> p t b n", t=2, b=2)
    acc = [b[:, :] for b in m.bank]

    def scores(n):
        v = sc[n % 2][:, :].rearrange("p (b n) -> p b n", b=2)[:, :, 0:2 * NKEY].rearrange("p b (h n) -> p b h n", h=2)
        return v[:, :, :, HD if its[n][0] == 0 else 0:NKEY]

    with nc.Block() as block:
        @block.gpsimd
        def _(pool):
            pool.iota(idist, pattern=[[-1, BAND]], base=HD, channel_multiplier=1).then_inc(iota_done, 1)
            pool.memset(vb[:, 0, 0:HD], 0.0).then_inc(vb_ready, 1)
            for i in range(NQ):
                lo = HD if i == 0 else 0
                c0 = META + P * i - HD + lo
                pool.tensor_copy(vb[:, i, lo:BAND], m.v1T[:, c0:c0 + BAND - lo]).then_inc(vb_ready, 1)
            pool.tensor_copy(vb[:, :, BAND:NKEY], bc(m.v1T[:, 0:META], 1, NQ)).then_inc(vb_ready, 1)
            for hg in range(NH // HG):
                hs = slice(HG * hg, HG * hg + HG)
                pool.wait_ge(bias_rounded, hg + 1)
                pool.tensor_tensor(bias_lo[:, hs], pbuf[hg], bias_hi[:, hs].bitcast(F32), ALU.subtract).then_inc(bias_split, 1)
            for n, (i, hg) in enumerate(its):
                s = slots[n % 4]
                pool.wait_ge(inverted, n + 1)
                p = pbuf[n % 4]
                pool.tensor_tensor(p, p, bc(s["den"], 2, NKEY), ALU.mult).then_inc(normed, 1)

        @block.vector
        def _(dve):
            c = Chain(dve, steps)
            dve.memset(kb[:, :, 0, 0:HD], 0.0)
            for i in range(NQ):
                lo = HD if i == 0 else 0
                c0 = META + P * i - HD + lo
                dve.tensor_copy(kb[:, :, i, lo:BAND], m.k1T[:, :, c0:c0 + BAND - lo])
            for kv in range(2):
                c.link(dve.tensor_copy(kb[:, kv, :, BAND:NKEY], bc(m.k1T[:, kv, 0:META], 1, NQ)))
            dve.wait_ge(iota_done, 1)
            c.link(dve.memset(dist, 0.0))
            c.link(dve.tensor_copy(dist[:, 0:BAND], idist))
            c.link(dve.scalar_tensor_tensor(dist[:, 0:BAND], dist[:, 0:BAND], -1.0, dist[:, 0:BAND], ALU.mult, ALU.min))
            dve.memset(dist[0:HD, 2 * HD:BAND], -MASK)
            c.link(dve.memset(dist[HD:P, 0:HD], -MASK))
            dve.tensor_copy(ident, m.ident[:, :])
            for hg in range(NH // HG):
                for j in range(HG):
                    ins = dve.tensor_scalar(pbuf[hg][:, place(j), :], dist, 2.0 ** (-8.0 * (HG * hg + j + 1) / NH), None, ALU.mult)
                c.link(ins)
                dve.tensor_copy(bias_hi[:, HG * hg:HG * hg + HG], pbuf[hg]).then_inc(bias_rounded, 1)
            for i in range(NQ // 2):
                for b, rows in enumerate((P, NB)):
                    dve.wait_ge(v_rounded, 2 * i + 2)
                    dve.tensor_tensor(v_lo[0:rows, 2 * i:2 * i + 2, b], v_rows(i)[0:rows, :, b],
                                      v_hi[0:rows, 2 * i:2 * i + 2, b].bitcast(F32), ALU.subtract).then_inc(v_split, 1)

            for n in range(NI + 4):
                if n < NI:
                    i, hg = its[n]
                    s = slots[n % 4]
                    p = pbuf[n % 4]
                    dve.wait_ge(scored, n + 1)
                    if n >= 4:
                        dve.wait_ge(turned, n - 3)
                    if i == 0:
                        dve.memset(p[:, :, 0:HD], 0.0)
                    c.link(dve.tensor_reduce(s["mx"].rearrange("p (b h) -> p b h", b=2), scores(n), AX_X, ALU.max))
                    c.link(dve.scalar_tensor_tensor(s["nm"], s["mx"], -1.0, m.nsinks[:, HG * hg:HG * hg + HG],
                                                    ALU.mult, ALU.min))
                    dve.tensor_tensor(s["es"], m.sinks[:, HG * hg:HG * hg + HG], s["nm"], ALU.add).then_inc(maxed, 1)
                if 0 <= n - 1 < NI:
                    i, hg = its[n - 1]
                    s = slots[(n - 1) % 4]
                    dve.wait_ge(exped, HG * n)
                    dve.wait_ge(sink_exped, n)
                    c.link(dve.tensor_tensor(s["den"], s["den"], s["es"], ALU.add))
                    dve.reciprocal(s["den"], s["den"]).then_inc(inverted, 1)
                if 0 <= n - 3 < NI:
                    k = n - 3
                    if k >= 2:
                        dve.wait_ge(weighed, k - 1)
                    for b, (src, rows) in enumerate(pt):
                        dve.wait_ge(pt_rounded, 2 * k + b + 1)
                        dve.tensor_tensor(pt_lo[k % 2][0:rows, b], src[0:rows, :], pt_hi[k % 2][0:rows, b].bitcast(F32),
                                          ALU.subtract).then_inc(pt_split, 1)
                if 0 <= n - 4 < NI:
                    k = n - 4
                    i, hg = its[k]
                    dve.wait_ge(weighed, k + 1)
                    for e in range(2):
                        g = m.mixT[HD * e:HD * e + HD, 2 * hg:2 * hg + 2, META + P * i:META + P * i + P]
                        o = acc[k % 2][0:HD, :].rearrange("p (a e q) -> p e a q", a=2, e=2)[:, e]
                        dve.tensor_tensor(g, g, o, ALU.mult).then_inc(gated, 1)

        @block.scalar
        def _(act):
            for i in range(NQ // 2):
                act.wait_ge(vt_filled, i + 1)
                for b, rows in enumerate((P, NB)):
                    act.activation(v_hi[0:rows, 2 * i:2 * i + 2, b], v_rows(i)[0:rows, :, b], ACT.Copy).then_inc(v_rounded, 1)
            for n in range(NI + 3):
                if n >= 3:
                    k = n - 3
                    act.wait_ge(turned, k + 1)
                    if k >= 2:
                        act.wait_ge(weighed, k - 1)
                    for b, (src, rows) in enumerate(pt):
                        act.activation(pt_hi[k % 2][0:rows, b], src[0:rows, :], ACT.Copy).then_inc(pt_rounded, 1)
                if n < NI:
                    s = slots[n % 4]
                    p = pbuf[n % 4]
                    act.wait_ge(maxed, n + 1)
                    if n >= 4:
                        act.wait_ge(normed, n - 3)
                    k0 = HD if its[n][0] == 0 else 0
                    for j in range(HG):
                        act.activation(p[:, j, k0:NKEY], scores(n)[:, j // 2, j % 2], ACT.Exp, bias=s["nm"][:, j:j + 1],
                                       accum_out=s["den"][:, j:j + 1]).then_inc(exped, 1)
                    act.activation(s["es"], s["es"], ACT.Exp).then_inc(sink_exped, 1)

        @block.tensor
        def _(pe):
            pe.wait_ge(vb_ready, NQ + 2)
            for i in range(NQ):
                dst = v_rows(i // 2)[:, i % 2]
                nc.tensor.transpose(dst[:, 0], vb[:, i, 0:P], m.ident[:, :])
                last = nc.tensor.transpose(dst[0:NB, 1], vb[:, i, P:NKEY], m.ident[:, :])
                if i % 2:
                    last.then_inc(vt_filled, 1)
            def score(n):
                i, hg = its[n]
                if n < NH // HG:
                    pe.wait_ge(bias_split, n + 1)
                if n >= 2:
                    pe.wait_ge(exped, HG * (n - 1))
                for b in range(2):
                    h0 = HG * hg + 2 * b
                    parts = [bias_hi] if b else [bias_hi, bias_lo]
                    for part in parts:
                        nc.tensor.matmul(sc[n % 2][:, BANK * b:BANK * b + 2 * NKEY], ident,
                                         part[:, h0:h0 + 2, :].rearrange("p h n -> p (h n)"),
                                         start=part is bias_hi, stop=part is parts[-1])
                for j in range(HG):
                    h = HG * hg + j
                    r = slice(HD * (h % 2), HD * (h % 2) + HD)
                    o = BANK * (j % 2) + NKEY * (j // 2)
                    dst = sc[n % 2][:, o:o + NKEY]
                    last = nc.tensor.matmul(dst, m.q1T[r, h // 2, P * i:P * i + P], kb[r, h // 8, i, :],
                                            start=False, stop=True, skip_group_check=True)
                last.then_inc(scored, 1)

            def turn(n):
                pe.wait_ge(normed, n + 1)
                if n >= 1:
                    pe.wait_ge(pt_split, 2 * n)
                else:
                    pe.wait_ge(v_split, NQ)
                p = pbuf[n % 4]
                for j in range(HG):
                    nc.tensor.transpose(pta[:, P * j:P * j + P], p[:, place(j), 0:P], m.ident[:, :])
                    last = nc.tensor.transpose(ptb_ps[0:NB, P * j:P * j + P], p[:, place(j), P:NKEY], m.ident[:, :])
                last.then_inc(turned, 1)

            def weigh(n):
                i, hg = its[n]
                pe.wait_ge(pt_split, 2 * (n + 1))
                if n >= 2:
                    pe.wait_ge(gated, 2 * (n - 1))
                kv = slice(HD * (hg // 2), HD * (hg // 2) + HD)
                for b, rows in enumerate((P, NB)):
                    for k, (v, p) in enumerate(((v_hi, pt_hi), (v_lo, pt_hi), (v_hi, pt_lo))):
                        last = nc.tensor.matmul(acc[n % 2][0:HD, :], v[0:rows, i, b, kv], p[n % 2][0:rows, b],
                                                start=(b == 0 and k == 0), stop=(b == 1 and k == 2))
                last.then_inc(weighed, 1)

            for n in range(NI + 4):
                if n < NI:
                    score(n)
                if 0 <= n - 3 < NI:
                    turn(n - 3)
                if 0 <= n - 4 < NI:
                    weigh(n - 4)


def odd_out_stage(nc, m, a, out, area):
    NQ = NT - 1
    src = split_mix(m, area, 1)
    h1 = area.take("h1_frames_sb", NQ * D).rearrange("p (t n) -> p t n", t=NQ)
    h1_loaded = [m.sem("h1_loaded") for _ in range(4)]
    whi, wlo = out_weights(area, 1)
    names = [f"oo{n}" for n in range(4)]
    ring = m.ring(m.banks, ["dve"] * (4 * NQ))
    stored = m.sem("stored")
    xs = [m.sem(x) for x in ("mix_hi_act", "mix_hi_dve", "mix_lo_pool", "mix_lo_dve")]
    ws = [m.sem(x) for x in ("w_hi", "w_lo", "w_first_hi", "w_first")]
    for n in range(4):
        m.section_end[names[n]] = (ws[1], n) if n else (ws[3], 1)
    free = lambda n: (ring.filled, NQ * (n + 1))

    with nc.Block() as block:
        @block.tensor
        def _(pe):
            for n in range(4):
                wait_out_weights(pe, ws, n)
                for t in range(NQ):
                    c0 = META + P * t
                    out_product(nc, m, pe, ring, NQ * n + t, slice(c0, c0 + P), n, P, whi, wlo, xs, ws)

        @block.vector
        def _(dve):
            out_split_engines(m, None, dve, None, src, names, whi, wlo, xs, ws, free, META)
            for n in range(4):
                for t in range(NQ):
                    i = NQ * n + t
                    if n == 0 and t % 2 == 0:
                        dve.wait_ge(h1_loaded[t // 2], 16)
                    ring.wait_filled(dve, i)
                    x = h1[:, t, SEC * n:SEC * n + SEC]
                    dve.tensor_tensor(x, x, ring.bank(i)[:, 0:SEC], ALU.add).then_inc(ring.emptied["dve"], 1)

        @block.scalar
        def _(act):
            out_split_engines(m, act, None, None, src, names, whi, wlo, xs, ws, free, META)

        @block.gpsimd
        def _(pool):
            out_split_engines(m, None, None, pool, src, names, whi, wlo, xs, ws, free, META)

        @block.sync
        def _(sp):
            for i in range(4):
                sp.dma_start(h1[:, 2 * i:2 * i + 2, :], m.h1_dram[2 * P * i:2 * P * (i + 1), :]
                             .rearrange("(t p) n -> p t n", p=P)).then_inc(h1_loaded[i], 16)
            send_sections(m, sp, len(m.sections) - 1)
            for t in range(NQ):
                sp.wait_ge(ring.emptied["dve"], 3 * NQ + t + 1)
                sp.dma_start(out[0, P * t:P * t + P, :], h1[:, t, :]).then_inc(stored, 16)
            sp.wait_ge(stored, 16 * NQ)




_INS = ["x", "meta_tokens", "ev_norm", "ev_w_in", "ev_q_norm", "ev_k_norm", "ev_log_dt", "ev_a_re", "ev_a_im",
        "ev_b_re", "ev_b_im", "ev_c_re", "ev_c_im", "ev_d", "ev_w_glu", "ev_b_glu", "ev_w_out", "od_norm",
        "od_w_in", "od_q_norm", "od_k_norm", "od_sinks", "od_w_out"]


def kernel(**inputs):
    import numpy as _np
    import concourse.bacc as _bacc
    from concourse import mybir as _mybir
    from concourse.bass_utils import run_bass_kernel_spmd as _run

    nc = _bacc.Bacc("TRN2", target_bir_lowering=False, num_devices=1)
    arrays, aps = {}, {}
    for name in _INS:
        v = _np.ascontiguousarray(inputs[name])
        arrays[f"in_{name}_dram"] = v
        aps[name] = nc.dram_tensor(f"in_{name}_dram", v.shape, _mybir.dt.from_np(v.dtype), kind="ExternalInput").ap()
    out = nc.dram_tensor("out_0_dram", (1, 1024, 1024), _mybir.dt.float32, kind="ExternalOutput").ap()
    kernel_program(nc, aps, out)
    r = _run(nc, [arrays], core_ids=[0])
    return r.results[0]["out_0_dram"]
```
